# Optimizing a Trainium2 kernel written in Bass

```python
import math
import jax, jax.numpy as jnp
from jax import lax
import numpy as np

D_MODEL = 1024
BATCH = 1
SEQ = 256
DEPTH = 1

DA_HEADS = 4
DA_HEAD_DIM = 64
DA_WIDTH = DA_HEADS * 2 * DA_HEAD_DIM
SB_HEADS = 8
SB_HEAD_DIM = 64
SB_WIDTH = SB_HEADS * SB_HEAD_DIM
ROPE_THETA = 10000.0
Q_BLOCK = 128
IN_SIZES = (DA_WIDTH, DA_WIDTH, DA_WIDTH, SB_WIDTH, SB_WIDTH, SB_WIDTH, D_MODEL, D_MODEL)
IN_WIDTH = 3 * DA_WIDTH + 3 * SB_WIDTH + 2 * D_MODEL
N_EXPERTS = 32
TOP_K = 4
D_FF = D_MODEL
SWIGLU_LIMIT = 7.0
SWIGLU_ALPHA = 1.702
MOE_BLOCK = 256
NORM_EPS = 1e-5

kernel_name = "hybrid_diffattn_stickbreak_moe"

def rms_norm(x, g):
    xf = x.astype(jnp.float32)
    y = xf * lax.rsqrt(jnp.mean(xf * xf, axis=-1, keepdims=True) + NORM_EPS)
    return (y * g.astype(jnp.float32)).astype(x.dtype)

def rope_tables(seq, dim):
    inv = 1.0 / (ROPE_THETA ** (jnp.arange(0, dim, 2, dtype=jnp.float32) / dim))
    ang = jnp.arange(seq, dtype=jnp.float32)[:, None] * inv[None, :]
    return jnp.cos(ang), jnp.sin(ang)

def apply_rope(x, cos, sin):
    xf = x.astype(jnp.float32)
    x1, x2 = jnp.split(xf, 2, axis=-1)
    c = cos[None, :, None, :]
    s = sin[None, :, None, :]
    return jnp.concatenate([x1 * c - x2 * s, x2 * c + x1 * s], axis=-1).astype(x.dtype)

def to_blocks(t):
    b, s = t.shape[:2]
    return jnp.moveaxis(t.reshape(b, s // Q_BLOCK, Q_BLOCK, *t.shape[2:]), 1, 0)

def from_blocks(t):
    t = jnp.moveaxis(t, 0, 1)
    return t.reshape(t.shape[0], t.shape[1] * t.shape[2], *t.shape[3:])

def diff_attention(q, k, v, lam, lambda_init, subln_g):
    b, s = q.shape[:2]
    nb = s // Q_BLOCK
    scale = DA_HEAD_DIM ** -0.5
    k_pos = jnp.arange(s)

    def block(args):
        qb, i = args
        q_pos = i * Q_BLOCK + jnp.arange(Q_BLOCK)
        sc = jnp.einsum('bqhd,bkhd->bhqk', qb, k, preferred_element_type=jnp.float32) * scale
        mask = k_pos[None, :] <= q_pos[:, None]
        p = jax.nn.softmax(jnp.where(mask, sc, -jnp.inf), axis=-1)
        p = p.reshape(b, DA_HEADS, 2, Q_BLOCK, s)
        w = p[:, :, 0] - lam * p[:, :, 1]
        return jnp.einsum('bhqk,bkhe->bqhe', w.astype(v.dtype), v)

    o = from_blocks(lax.map(block, (to_blocks(q), jnp.arange(nb))))
    o = rms_norm(o, subln_g) * (1.0 - lambda_init)
    return o.reshape(b, s, DA_WIDTH)

def stick_breaking_attention(q, k, v):
    b, s = q.shape[:2]
    nb = s // Q_BLOCK
    scale = SB_HEAD_DIM ** -0.5
    k_pos = jnp.arange(s)

    def block(args):
        qb, i = args
        q_pos = i * Q_BLOCK + jnp.arange(Q_BLOCK)
        z = jnp.einsum('bqhd,bkhd->bhqk', qb, k, preferred_element_type=jnp.float32) * scale
        mask = k_pos[None, :] < q_pos[:, None]
        log_1m = jnp.where(mask, jax.nn.log_sigmoid(-z), 0.0)
        suffix = lax.cumsum(log_1m, axis=3, reverse=True) - log_1m
        a = jnp.where(mask, jnp.exp(jax.nn.log_sigmoid(z) + suffix), 0.0)
        return jnp.einsum('bhqk,bkhd->bqhd', a.astype(v.dtype), v)

    o = from_blocks(lax.map(block, (to_blocks(q), jnp.arange(nb))))
    return o.reshape(b, s, SB_WIDTH)

def moe_ffn(h, w_router, b_router, w_gate, b_gate, w_up, b_up, w_down, b_down):
    n, d = h.shape
    logits = (h @ w_router + b_router).astype(jnp.float32)
    top_val, top_idx = lax.top_k(logits, TOP_K)
    gates = jax.nn.softmax(top_val, axis=-1).astype(h.dtype)
    m = n * TOP_K
    flat_e = top_idx.reshape(m)
    flat_tok = jnp.arange(m, dtype=jnp.int32) // TOP_K
    flat_g = gates.reshape(m)
    order = jnp.argsort(flat_e)
    sorted_e = flat_e[order]
    counts = jnp.bincount(flat_e, length=N_EXPERTS)
    padded = (counts + MOE_BLOCK - 1) // MOE_BLOCK * MOE_BLOCK
    starts = jnp.cumsum(counts) - counts
    pad_ends = jnp.cumsum(padded)
    pad_starts = pad_ends - padded
    dest = pad_starts[sorted_e] + jnp.arange(m, dtype=jnp.int32) - starts[sorted_e]
    n_blocks = (m + MOE_BLOCK - 1) // MOE_BLOCK + N_EXPERTS
    p_rows = n_blocks * MOE_BLOCK
    row_tok = jnp.zeros((p_rows,), jnp.int32).at[dest].set(flat_tok[order])
    row_gate = jnp.zeros((p_rows,), h.dtype).at[dest].set(flat_g[order])
    blk_e = jnp.minimum(
        jnp.searchsorted(pad_ends, jnp.arange(n_blocks, dtype=jnp.int32) * MOE_BLOCK, side='right'),
        N_EXPERTS - 1)
    xs = h[row_tok].reshape(n_blocks, MOE_BLOCK, d)

    def expert_block(args):
        xb, e = args
        g = xb @ w_gate[e] + b_gate[e]
        u = xb @ w_up[e] + b_up[e]
        g = jnp.minimum(g, SWIGLU_LIMIT)
        u = jnp.clip(u, -SWIGLU_LIMIT, SWIGLU_LIMIT)
        glu = g * jax.nn.sigmoid(SWIGLU_ALPHA * g)
        return ((u + 1.0) * glu) @ w_down[e] + b_down[e]

    out = lax.map(expert_block, (xs, blk_e)).reshape(p_rows, d)
    return jnp.zeros_like(h).at[row_tok].add(out * row_gate[:, None])

def setup_inputs(seed: int = 0) -> dict:
    key = jax.random.key(seed)
    ks = jax.random.split(key, 24)
    f32 = jnp.float32
    L, D, E, F = DEPTH, D_MODEL, N_EXPERTS, D_FF

    def nrm(k, shape, scale):
        return jax.random.normal(k, shape, f32) * scale

    return {
        "x": nrm(ks[0], (BATCH, SEQ, D), 1.0),
        "norm_mix_g": 1.0 + nrm(ks[1], (L, D), 0.01),
        "w_in": nrm(ks[2], (L, D, IN_WIDTH), D ** -0.5),
        "lambda_q1": nrm(ks[3], (L, DA_HEAD_DIM), 0.1),
        "lambda_k1": nrm(ks[4], (L, DA_HEAD_DIM), 0.1),
        "lambda_q2": nrm(ks[5], (L, DA_HEAD_DIM), 0.1),
        "lambda_k2": nrm(ks[6], (L, DA_HEAD_DIM), 0.1),
        "da_subln_g": 1.0 + nrm(ks[7], (L, 2 * DA_HEAD_DIM), 0.01),
        "w_da_out": nrm(ks[8], (L, DA_WIDTH, D), DA_WIDTH ** -0.5),
        "w_sb_out": nrm(ks[9], (L, SB_WIDTH, D), SB_WIDTH ** -0.5),
        "w_o": nrm(ks[10], (L, D, D), D ** -0.5),
        "norm_ffn_g": 1.0 + nrm(ks[11], (L, D), 0.01),
        "w_router": nrm(ks[12], (L, D, E), D ** -0.5),
        "b_router": nrm(ks[13], (L, E), 0.01),
        "w_gate": nrm(ks[14], (L, E, D, F), D ** -0.5),
        "b_gate": nrm(ks[15], (L, E, F), 0.01),
        "w_up": nrm(ks[16], (L, E, D, F), D ** -0.5),
        "b_up": nrm(ks[17], (L, E, F), 0.01),
        "w_down": nrm(ks[18], (L, E, F, D), F ** -0.5),
        "b_down": nrm(ks[19], (L, E, D), 0.01),
        "norm_final_g": 1.0 + nrm(ks[20], (D,), 0.01),
    }

def reference(x, norm_mix_g, w_in, lambda_q1, lambda_k1, lambda_q2, lambda_k2, da_subln_g,
              w_da_out, w_sb_out, w_o, norm_ffn_g, w_router, b_router, w_gate, b_gate,
              w_up, b_up, w_down, b_down, norm_final_g):
    b, s, d = x.shape
    cos, sin = rope_tables(s, DA_HEAD_DIM)
    split_points = np.cumsum(IN_SIZES)[:-1].tolist()
    for l in range(DEPTH):
        lambda_init = 0.8 - 0.6 * math.exp(-0.3 * l)
        h = rms_norm(x, norm_mix_g[l])
        proj = h @ w_in[l]
        qa, ka, va, qb, kb, vb, ga, gb = jnp.split(proj, split_points, axis=-1)
        qa = apply_rope(qa.reshape(b, s, 2 * DA_HEADS, DA_HEAD_DIM), cos, sin)
        ka = apply_rope(ka.reshape(b, s, 2 * DA_HEADS, DA_HEAD_DIM), cos, sin)
        va = va.reshape(b, s, DA_HEADS, 2 * DA_HEAD_DIM)
        lam = (jnp.exp(jnp.sum(lambda_q1[l].astype(jnp.float32) * lambda_k1[l].astype(jnp.float32)))
               - jnp.exp(jnp.sum(lambda_q2[l].astype(jnp.float32) * lambda_k2[l].astype(jnp.float32)))
               + lambda_init)
        ya = diff_attention(qa, ka, va, lam, lambda_init, da_subln_g[l]) @ w_da_out[l]
        yb = stick_breaking_attention(qb.reshape(b, s, SB_HEADS, SB_HEAD_DIM),
                                      kb.reshape(b, s, SB_HEADS, SB_HEAD_DIM),
                                      vb.reshape(b, s, SB_HEADS, SB_HEAD_DIM)) @ w_sb_out[l]
        mix = jax.nn.sigmoid(ga) * ya + jax.nn.sigmoid(gb) * yb
        x = x + mix @ w_o[l]
        h = rms_norm(x, norm_ffn_g[l]).reshape(b * s, d)
        y = moe_ffn(h, w_router[l], b_router[l], w_gate[l], b_gate[l], w_up[l], b_up[l],
                    w_down[l], b_down[l])
        x = x + y.reshape(b, s, d)
    return rms_norm(x, norm_final_g)


_drawn_inputs = setup_inputs


def setup_inputs(seed=0):
    import zlib

    import numpy as np

    out = dict(_drawn_inputs(seed))
    spreads = {}
    factors = {'lambda_q2': 25.781,
     'da_subln_g': 3.667,
     'b_gate': 21.592,
     'b_up': 31.649,
     'b_down': 51.857,
     'norm_final_g': 200.0,
     'norm_ffn_g': 3.603,
     'b_router': 2.703}
    for name, (base, spread) in spreads.items():
        noise = np.random.default_rng([zlib.crc32(name.encode()), seed]).standard_normal(out[name].shape)
        drawn = base * np.exp(spread * noise) if base else spread * noise
        out[name] = __import__('jax').numpy.asarray(drawn.astype(out[name].dtype))
    for name, factor in factors.items():
        out[name] = (out[name] * factor).astype(out[name].dtype)
    return out
```

```python
from contextlib import ExitStack

import numpy as np

import concourse.bass as bass
import concourse.mybir as mybir
from concourse.alu_op_type import AluOpType as ALU

F32 = mybir.dt.float32
BF16 = mybir.dt.bfloat16
I32 = mybir.dt.int32
ACT = mybir.ActivationFunctionType
AX = mybir.AxisListType

P = 128
T = 256
NT = T // P
D = 1024
KC = D // P
HD = 64
HEADS = 8
DA_HEADS = 4
W512 = 512
E = 32
FF = 1024
TOP_K = 4
SLOTS = T // 4
ROUNDS = T // SLOTS
PAIRS = E // 2
PAIRS_PER_ITER = 2
ITERS = PAIRS // PAIRS_PER_ITER
RING = 8
SLOT_COLS = 4096
HEAD_LOADS = 14
LOADS_PER_PAIR = 12
LOADS_PER_ITER = PAIRS_PER_ITER * LOADS_PER_PAIR
SLOTS_AT_ALL = RING + 2
ROWS2 = 2 * D
BQ = FF // (P // E)
NORM_EPS = 1e-5
LAMBDA_INIT = 0.2
LIMIT = 7.0
ALPHA = 1.702
Q_SCALE = HD ** -0.5
MASKED = -1e30
BLOCKS = 3 * P

C_ID, C_ROPE, C_IOTA, C_TRI, C_ONE, C_MDA, C_MSB, C_KEEP = 0, 128, 320, 384, 512, 640, 896, 1024
C_SU, C_ONEP, C_E3 = 1024, 1152, 1280
N_ROUND_COLS = ROUNDS * E + 2
C_END = C_E3 + N_ROUND_COLS


def constants():
    c = np.zeros((P, C_END), np.float32)
    i = np.arange(P)
    c[:, C_ID:C_ID + P] = np.eye(P)
    c[:, C_TRI:C_TRI + P] = -(i[:, None] >= i[None, :]).astype(np.float32)
    c[:, C_ONE:C_ONE + P] = -1.0
    c[:, C_MDA + P:C_MDA + 2 * P] = np.where(i[None, :] <= i[:, None], 0.0, MASKED)
    c[:, C_MSB:C_MSB + P] = np.where(i[:, None] < i[None, :], 0.0, MASKED)
    inv = (1.0 / (np.float32(10000.0) ** (np.arange(0, HD, 2, dtype=np.float32) / np.float32(HD)))).astype(np.float32)
    ang = np.arange(T, dtype=np.float32)[:, None] * inv[None, :]
    rope = np.stack([np.cos(ang), np.sin(ang), -np.sin(ang)], 1).reshape(NT, P, 3, HD // 2)
    c[:, C_ROPE:C_ROPE + 192] = rope.transpose(1, 0, 2, 3).reshape(P, 192)
    c[:, C_IOTA:C_IOTA + SLOTS] = np.arange(SLOTS)[None, :]
    c[:, C_SU:C_SU + P] = (i[:, None] < i[None, :])
    c[:, C_ONEP:C_ONEP + P] = 1.0
    c[:, C_E3:C_E3 + N_ROUND_COLS] = (i[:, None] % E == np.arange(N_ROUND_COLS)[None, :] % E)
    return c


class Steps:

    def __init__(self, engine, semaphore, base=0):
        self.engine, self.semaphore, self.base, self.n = engine, semaphore, base, 0

    def step(self, instruction):
        instruction.then_inc(self.semaphore, 1)
        self.n += 1

    def settle(self):
        self.engine.wait_ge(self.semaphore, self.base + self.n)


QB, KB, VB, QA, KA, TRQ, VA, TRK, GA0, GA1, GB0, GB1 = range(12)
STEP_OF_SLOT = [QB, KB, VB, QA, KA, VA, GA0, GA1, GB0, GB1]
STEP_SLOT = {QB: 0, KB: 1, VB: 2, QA: 3, KA: 4, VA: 5, GA0: 6, GA1: 7, GB0: 8, GB1: 9}
STEP_COLS = {QA: 0, KA: 512, VA: 1024, QB: 1536, KB: 2048, VB: 2560, GA0: 3072, GA1: 3584, GB0: 4096, GB1: 4608}
EVACUATIONS = {QB: 2, KB: 1, VB: 1, QA: 1, KA: 1, TRQ: 2, VA: 1, TRK: 2, GA0: 1, GA1: 1, GB0: 1, GB1: 1}
DVE_STEPS_PER_ITER = 4


def slot_plan():
    fixed = [(HEAD_LOADS + k) % RING for k in range(4)]
    turns = [(HEAD_LOADS + k) % RING for k in range(4, 8)] + [RING, RING + 1]
    slot_of = []
    n_turned = 0
    for p in range(LOADS_PER_ITER):
        if p % 8 < 4:
            slot_of.append(fixed[p % 8])
        else:
            slot_of.append(turns[n_turned % len(turns)])
            n_turned += 1
    assert n_turned % len(turns) == 0
    before = []
    for p in range(LOADS_PER_ITER):
        q = p - 1
        while slot_of[q % LOADS_PER_ITER] != slot_of[p]:
            q -= 1
        before.append(q)
    return slot_of, before


SLOT_OF, USED_BEFORE = slot_plan()
FIRST_LOADS = [0, 1, 2, 3, 4, 5, SLOT_OF.index(RING), 6, 7, SLOT_OF.index(RING + 1)]


def build(nc, x_d, norm_mix_g, w_in, lam_q1, lam_k1, lam_q2, lam_k2, subln_g, w_da_out, w_sb_out, w_o,
          norm_ffn_g, w_router, b_router, w_gate, b_gate, w_up, b_up, w_down, b_down, norm_final_g, const_d, out_d):
    ctx = ExitStack()
    with ctx:
        def sb(name, cols, dt=F32):
            return ctx.enter_context(nc.sbuf_tensor(name, [P, cols], dt))

        def sem(name):
            return ctx.enter_context(nc.semaphore(name))

        ring = sb("ring", RING * SLOT_COLS)

        def slot(s, rows, cols):
            return ring[:, s * SLOT_COLS:(s + 1) * SLOT_COLS].rearrange("p (c n) -> p c n", c=rows)

        def expert_part(s, k):
            if s < RING:
                lo = s * SLOT_COLS + k * ROWS2
                return ring[:, lo:lo + ROWS2]
            if s == RING:
                return r_qk[:, k * ROWS2:(k + 1) * ROWS2]
            return (r_a, r_kvc)[k][:, D:D + ROWS2]

        x_t = sb("x", NT * D)
        r_a = sb("region_a", 4096)
        r_a1 = r_a[:, 0:2048]
        r_a2 = r_a[:, 2048:4096]
        r_kvc = sb("region_kvc", 2048 + 640 + 512)
        r_kv = r_kvc[:, 0:2048]
        cst2 = r_kvc[:, 2048:2688]
        r_tb = r_kvc[:, 2688:3200]
        r_qk = sb("region_qk", SLOT_COLS)
        r_qa = r_qk[:, 0:2048]
        r_ka = r_qk[:, 2048:3072]
        r_va = sb("region_va", 1024)
        r_w = sb("region_w", 3072)
        r_wt = sb("region_wt", 2 * BLOCKS)
        r_o = sb("region_o", 1024)
        r_ob = sb("region_ob", 1024)
        cst = sb("cst", C_TRI)
        su_b = sb("su_b", P, BF16)
        one_b = sb("one_b", P, BF16)
        e3_b = sb("e3_b", N_ROUND_COLS, BF16)
        g_mix = sb("g_mix", KC)
        g_ffn = sb("g_ffn", KC)
        g_sub = sb("g_sub", 1)
        wr = sb("wr", KC * E)
        br = sb("br", E)
        lam_in = sb("lam_in", 4 * HD)
        gB = sb("gB", D)[:, :]
        bias3 = sb("bias3", 3 * D, BF16)[:, :].rearrange("p (w n) -> p w n", w=3)
        small = sb("small", 128)

        x3 = x_t[:, :].rearrange("p (a n) -> p a n", a=NT)
        xn3 = r_kv[:, :].rearrange("p (a n) -> p a n", a=NT)
        hT = r_a1[:, :].rearrange("p (c t) -> p c t", c=KC)
        mixT = hT
        h32 = [r[:, 0:D].rearrange("p (c m) -> p c m", c=KC) for r in (r_a1, r_kv)]
        g_s, u_s = r_a1[:, 0:D], r_va[:, :]
        qbz = r_a2[:, :].rearrange("p (h t) -> p h t", h=HEADS)
        sga = r_a2[:, :].rearrange("p (c t) -> p c t", c=KC)
        hTr = [r_a2[:, a * D:(a + 1) * D].rearrange("p (c t) -> p c t", c=KC) for a in range(NT)]
        xT = r_a2[:, D:2 * D].rearrange("p (c s) -> p c s", c=KC)
        kbT = r_kv[:, 0:1024].rearrange("p (c t) -> p c t", c=4)
        vb3 = r_kv[:, 1024:2048].rearrange("p (a n) -> p a n", a=NT)
        gfin = gB
        o_s = sg_s = r_kv[:, 0:1024]
        qaz = r_qa[:, :].rearrange("p (h t) -> p h t", h=HEADS)
        sgb = r_qa[:, :].rearrange("p (c t) -> p c t", c=KC)
        braw = r_ob[:, 0:3 * BQ].rearrange("p (w n) -> p w n", w=3)
        bpart = [r[:, lo:lo + 3 * BQ // 2].bitcast(BF16).rearrange("p (w n) -> p w n", w=3)
                 for r, lo in ((r_tb, 0), (r_wt, 0), (r_wt, 3 * BQ // 2))]
        kaT = r_ka[:, :].rearrange("p (c t) -> p c t", c=4)
        va3 = r_va[:, :].rearrange("p (a n) -> p a n", a=NT)
        hTm = r_va[:, :].rearrange("p (c s) -> p c s", c=KC)
        zb = r_w[:, 0:4 * BLOCKS].rearrange("p (h n) -> p h n", h=4)
        sp = r_w[:, 4 * BLOCKS:8 * BLOCKS].rearrange("p (h n) -> p h n", h=4)
        pb = r_w[:, :].rearrange("p (h n) -> p h n", h=HEADS)
        on3 = r_w[:, 0:1024].rearrange("p (a n) -> p a n", a=NT)
        h3 = r_w[:, :].bitcast(BF16).rearrange("p (a w c m) -> p a w c m", a=NT, w=3, c=KC)
        wT = r_wt[:, :].rearrange("p (h n) -> p h n", h=2)
        rot = r_o[:, :].rearrange("p (a n) -> p a n", a=NT)
        oT = r_o[:, :].rearrange("p (h t) -> p h t", h=DA_HEADS)
        obT = r_ob[:, :].rearrange("p (h t) -> p h t", h=4)
        ident = cst[:, C_ID:C_ID + P]
        tri_neg = cst2[:, C_TRI - C_TRI:C_ONE - C_TRI]
        one_neg = cst2[:, C_ONE - C_TRI:C_MDA - C_TRI]
        mask_da = cst2[:, C_MDA - C_TRI:C_MSB - C_TRI]
        mask_sb = cst2[:, C_MSB - C_TRI:C_KEEP - C_TRI]
        rope = cst[:, C_ROPE:C_ROPE + 192].rearrange("p (a w d) -> p a w d", a=NT, w=3)
        iota = cst[:, C_IOTA:C_IOTA + SLOTS]
        wr3 = wr[:, :].rearrange("p (c e) -> p c e", c=KC)

        ssq, var, std, rstd = (small[:, 2 * k:2 * k + 2] for k in range(4))
        lam4, lamv = small[:, 8:12], small[:, 12:14]
        g_sub8 = small[:, 14:15]
        mx = small[:, 16:32].rearrange("p (h a) -> p h a", a=2)
        nmx = small[:, 32:48].rearrange("p (h a) -> p h a", a=2)
        den = small[:, 48:64].rearrange("p (h a) -> p h a", a=2)
        rden = small[:, 64:80].rearrange("p (h a) -> p h a", a=2)
        c2 = small[:, 80:88].rearrange("p (h a) -> p h a", a=2)
        ossq, orstd = small[:, 88:96], small[:, 96:104]
        nrd = small[:, 104:108]
        nr_i = sb("nr_i", 1, I32)

        def carve(region, start, cols):
            return region[:, start:start + cols]

        lT = carve(r_o, 0, 256)
        lg = carve(r_o, 256, 64).rearrange("p (a e) -> p a e", a=NT)
        top8 = carve(r_o, 320, 16).rearrange("p (a e) -> p a e", a=NT)
        eq = carve(r_o, 336, 64).rearrange("p (a e) -> p a e", a=NT)
        gt = carve(r_o, 400, 64).rearrange("p (a e) -> p a e", a=NT)
        cum = carve(r_o, 464, 64).rearrange("p (a e) -> p a e", a=NT)
        mask = carve(r_o, 528, 64).rearrange("p (a e) -> p a e", a=NT)
        ex = carve(r_o, 592, 64).rearrange("p (a e) -> p a e", a=NT)
        gates = carve(r_o, 656, 64).rearrange("p (a e) -> p a e", a=NT)
        mask_b = carve(r_o, 720, 32).bitcast(BF16).rearrange("p (a e) -> p a e", a=NT)
        rt = carve(r_o, 752, 16)
        ones_row = sb("ones_row", E)[:, :]
        rkx = carve(r_ob, 0, 2 * N_ROUND_COLS).rearrange("p (a n) -> p a n", a=NT)
        gx = carve(r_wt, 0, 2 * N_ROUND_COLS).rearrange("p (a n) -> p a n", a=NT)
        rk1 = carve(r_wt, 264, 64).rearrange("p (a e) -> p a e", a=NT)
        s_sel = carve(r_ob, 264, 128).bitcast(BF16).rearrange("p (a s) -> p a s", a=NT)
        gs = carve(r_ob, 392, 256).rearrange("p (a s) -> p a s", a=NT)
        g_T = carve(r_ob, 648, 256)
        oh = [carve(r_wt, 328 + 64 * q, 64).bitcast(BF16) for q in range(2)]

        ps = ctx.enter_context(nc.psum_tensor("ps", [P, 8 * W512], F32))

        def bank(b, n=1):
            return ps[:, b * W512:(b + n) * W512]

        G_B, U_B, O_B, T_B = 0, 2, 4, 6

        slot_loaded = [sem(f"slot_loaded{s}") for s in range(SLOTS_AT_ALL)]
        load_used = sem("load_used")
        ld_x = [sem(f"ld_x{a}") for a in range(NT)]
        ld_id, ld_gmix, ld_const, ld_const2 = sem("ld_id"), sem("ld_gmix"), sem("ld_const"), sem("ld_const2")
        ld_lam, ld_gsub, ld_router = sem("ld_lam"), sem("ld_gsub"), sem("ld_router")
        ld_gB, ld_gfin, ld_bias, ld_bias3 = sem("ld_gB"), sem("ld_gfin"), sem("ld_bias"), sem("ld_bias3")
        stored = sem("stored")
        const_cast, zeroed = sem("const_cast"), sem("zeroed")
        dve_own, act_own = sem("dve_own"), sem("act_own")
        ms_ready, std_ready, rstd_ready = sem("ms_ready"), sem("std_ready"), sem("rstd_ready")
        xn_ready, xn1_ready, hT_tr = sem("xn_ready"), sem("xn1_ready"), sem("hT_tr")
        hT_dve, hT_act = sem("hT_dve"), sem("hT_act")
        lam_dot, lam_exp = sem("lam_dot"), sem("lam_exp")
        step_done = sem("step_done")
        evac = [sem(f"evac{i}") for i in range(12)]
        rope_done = sem("rope_done")
        sb_z, sb_abs, sb_ln, sb_sp, sb_r = sem("sb_z"), sem("sb_abs"), sem("sb_ln"), sem("sb_sp"), sem("sb_r")
        sb_arg, sb_a, sb_o, sb_ev = sem("sb_arg"), sem("sb_a"), sem("sb_o"), sem("sb_ev")
        da_s, da_read, da_nm, da_e, da_w = sem("da_s"), sem("da_read"), sem("da_nm"), sem("da_e"), sem("da_w")
        da_t, da_wt, da_o, da_ssq = sem("da_t"), sem("da_wt"), sem("da_o"), sem("da_ssq")
        da_var, da_std, on_ready, tro, oT_act, oT_dve = (sem(n) for n in (
            "da_var", "da_std", "on_ready", "tro", "oT_act", "oT_dve"))
        yb_done, ya_done, mix_ready, wo_done, x1 = (sem(n) for n in ("yb_done", "ya_done", "mix_ready", "wo_done", "x1"))
        tx_done, hTr_dve, hTr_act, rt_done, lT_ready, rt_tr = (sem(n) for n in (
            "tx_done", "hTr_dve", "hTr_act", "rt_done", "lT_ready", "rt_tr"))
        ms2_ready, std2_ready, neg_top, ex_ready, mask_ready, rk_done = (sem(n) for n in (
            "ms2_ready", "std2_ready", "neg_top", "ex_ready", "mask_ready", "rk_done"))
        h_full, h_p1, h_r1, h_p2, h_ready = (sem(n) for n in ("h_full", "h_p1", "h_r1", "h_p2", "h_ready"))
        bias_parts, gates_ready, nr_ready, ssq1_ready, ssq2_ready = (sem(n) for n in (
            "bias_parts", "gates_ready", "nr_ready", "ssq1_ready", "ssq2_ready"))
        sel_ready, gat_done, xT_ready, gate_done, up_done = (sem(n) for n in (
            "sel_ready", "gat_done", "xT_ready", "gate_done", "up_done"))
        g_clipped, gs_ready, gt_done, gt_ready, sig_ready, act_ready = (sem(n) for n in (
            "g_clipped", "gs_ready", "gt_done", "gt_ready", "sig_ready", "act_ready"))
        ht_done, hT_ready, down_done, o_ready, sc_done, y_added = (sem(n) for n in (
            "ht_done", "hT_ready", "down_done", "o_ready", "sc_done", "y_added"))
        fin_ms, fin_std, fin_done = sem("fin_ms"), sem("fin_std"), sem("fin_done")

        wg_v = w_gate.rearrange("e (p c) n -> e p (c n)", c=KC)
        wu_v = w_up.rearrange("e (p c) n -> e p (c n)", c=KC)
        wd_v = w_down.rearrange("e (h p c) n -> e h p (c n)", h=2, c=4)
        w_in_v = w_in.rearrange("(p c) n -> p c n", c=KC)

        def rounds_after_first(engine, body):
            engine.wait_ge(nr_ready, 1)
            rounds = engine.value_load(nr_i[0:1, 0:1], min_val=1, max_val=ROUNDS)
            with engine.If(rounds > 1):
                with engine.Fori(1, rounds) as r:
                    with engine.Fori(0, ITERS) as i:
                        body(i, r * ITERS + i)
            return rounds

        block = ctx.enter_context(nc.Block())

        @block.sync
        def _(sp_):
            for a in range(NT):
                sp_.dma_start(x3[:, a, :], x_d[a * P:(a + 1) * P, :]).then_inc(ld_x[a], 16)

            def small_loads():
                sp_.dma_start(cst2, const_d[:, C_TRI:C_KEEP]).then_inc(ld_const, 16)
                sp_.dma_start(cst[:, C_ROPE:C_TRI], const_d[:, C_ROPE:C_TRI]).then_inc(ld_const, 16)
                sp_.dma_start(r_w[:, 0:C_END - C_KEEP], const_d[:, C_KEEP:C_END]).then_inc(ld_const2, 16)
                for w, b in enumerate((b_gate, b_up, b_down)):
                    sp_.dma_start(braw[:, w, :], b.rearrange("e (q n) -> (e q) n", n=BQ)).then_inc(ld_bias, 16)
                for k, v in enumerate((lam_q1, lam_k1, lam_q2, lam_k2)):
                    sp_.dma_start(lam_in[:, k * HD:(k + 1) * HD], v[0].partition_broadcast(P)).then_inc(ld_lam, 16)
                sp_.dma_start(g_sub[:, :], subln_g[0].rearrange("(p c) -> p c", c=1)).then_inc(ld_gsub, 16)

            def later_loads():
                sp_.dma_start(g_ffn[:, :], norm_ffn_g[0].rearrange("(p c) -> p c", c=KC)).then_inc(ld_router, 16)
                sp_.dma_start(br[:, :], b_router[0].partition_broadcast(P)).then_inc(ld_router, 16)
                sp_.dma_start(wr3, w_router.rearrange("(p c) e -> p c e", c=KC)).then_inc(ld_router, 16)
                sp_.dma_start(gB, norm_ffn_g[0].partition_broadcast(P)).then_inc(ld_gB, 16)
                sp_.wait_ge(bias_parts, 5)
                for k in range(3):
                    for q in range(P // E):
                        sp_.dma_start(bias3[k * E:(k + 1) * E, :, q * BQ:(q + 1) * BQ],
                                      bpart[k][q:P:P // E, :, :]).then_inc(ld_bias3, 16)

            for n in range(HEAD_LOADS):
                if n == 2:
                    small_loads()
                if n == RING:
                    later_loads()
                s = n % RING
                if n >= RING:
                    sp_.wait_ge(step_done, STEP_OF_SLOT[n - RING] + 1)
                if n < 10:
                    col = STEP_COLS[STEP_OF_SLOT[n]]
                    sp_.dma_start(slot(s, KC, W512), w_in_v[:, :, col:col + W512]).then_inc(slot_loaded[s], 16)
                else:
                    src = (w_sb_out, w_da_out, w_o[0:W512, :], w_o[W512:D, :])[n - 10]
                    sp_.dma_start(slot(s, 4, D), src.rearrange("(c p) n -> p c n", c=4)).then_inc(slot_loaded[s], 16)

            def load(i, p):
                e = i * (2 * PAIRS_PER_ITER) + 2 * (p // LOADS_PER_PAIR)
                m, s = p % LOADS_PER_PAIR, SLOT_OF[p]
                if m < 8:
                    src = (wg_v, wu_v)[m // 4][bass.ds(e, 2), :, (m % 4) * ROWS2:(m % 4 + 1) * ROWS2]
                else:
                    src = wd_v[bass.ds(e, 2), (m - 8) // 2, :, (m % 2) * ROWS2:(m % 2 + 1) * ROWS2]
                if s <= RING:
                    dst = slot(s, 2, ROWS2) if s < RING else r_qk[:, :].rearrange("p (k n) -> p k n", k=2)
                    sp_.dma_start(dst, src.rearrange("k p n -> p k n")).then_inc(slot_loaded[s], 16)
                else:
                    for k in range(2):
                        sp_.dma_start(expert_part(s, k), src[k]).then_inc(slot_loaded[s], 16)

            def load_iteration(i, it):
                for p in range(LOADS_PER_ITER):
                    sp_.wait_ge(load_used, it * LOADS_PER_ITER + USED_BEFORE[p] + 1)
                    load(i, p)

            slot_free = {0: (step_done, GA0 + 1), 1: (step_done, GA1 + 1), 2: (step_done, GB0 + 1),
                         3: (step_done, GB1 + 1), 4: (yb_done, 4), 5: (ya_done, 4),
                         SLOT_OF.index(RING): (mix_ready, 4),
                         6: (rt_done, 1), 7: (wo_done, NT), SLOT_OF.index(RING + 1): (wo_done, NT)}
            for p in FIRST_LOADS:
                sp_.wait_ge(*slot_free[p])
                load(0, p)
            sp_.wait_ge(h_full, NT)
            sp_.dma_start(gfin, norm_final_g.partition_broadcast(P)).then_inc(ld_gfin, 16)
            for p in range(LOADS_PER_ITER):
                if p not in FIRST_LOADS:
                    sp_.wait_ge(load_used, USED_BEFORE[p] + 1)
                    load(0, p)
            with sp_.Fori(1, ITERS) as i:
                load_iteration(i, i)
            rounds_after_first(sp_, load_iteration)
            for a in range(NT):
                sp_.wait_ge(fin_done, a + 1)
                sp_.dma_start(out_d[a * P:(a + 1) * P, :], x3[:, a, :]).then_inc(stored, 16)
            sp_.wait_ge(stored, 16 * NT)

        @block.gpsimd
        def _(pool):
            nc.gpsimd.memset(ones_row, 1.0).then_inc(zeroed, 1)
            nc.gpsimd.memset(qbz, 0.0).then_inc(zeroed, 1)
            nc.gpsimd.memset(qaz, 0.0).then_inc(zeroed, 1)
            pool.wait_ge(ld_const2, 16)
            stage = r_w[:, 0:C_END - C_KEEP]
            nc.gpsimd.tensor_copy(su_b[:, :], stage[:, C_SU - C_KEEP:C_SU - C_KEEP + P])
            nc.gpsimd.tensor_copy(one_b[:, :], stage[:, C_ONEP - C_KEEP:C_ONEP - C_KEEP + P])
            nc.gpsimd.tensor_copy(e3_b[:, :], stage[:, C_E3 - C_KEEP:C_END - C_KEEP]).then_inc(const_cast, 1)

            own = Steps(pool, bias_parts)
            pool.wait_ge(ld_bias, 16 * 3)
            own.step(nc.gpsimd.tensor_copy(bpart[0], braw))
            for k in (1, 2):
                own.settle()
                own.step(nc.gpsimd.tensor_tensor(braw, braw, bpart[k - 1], ALU.subtract))
                own.settle()
                own.step(nc.gpsimd.tensor_copy(bpart[k], braw))
            assert own.n == 5

        @block.scalar
        def _(act):
            own = Steps(act, act_own)
            act.dma_start(ident, const_d[:, C_ID:C_ID + P]).then_inc(ld_id, 16)
            act.dma_start(g_mix[:, :], norm_mix_g[0].rearrange("(p c) -> p c", c=KC)).then_inc(ld_gmix, 16)
            act.wait_ge(zeroed, 1)
            nc.scalar.activation(std, ones_row[:, 0:2], ACT.Sqrt)

            act.wait_ge(ld_x[1], 16)
            nc.scalar.activation(r_a1[:, D:2 * D], x3[:, 1, :], ACT.Square, accum_out=ssq[:, 1:2]).then_inc(ssq1_ready, 1)
            act.wait_ge(ms_ready, 1)
            nc.scalar.activation(std, var, ACT.Sqrt).then_inc(std_ready, 1)
            act.wait_ge(rstd_ready, 1)
            nc.scalar.activation(xn3[:, 1, :], x3[:, 1, :], ACT.Copy, scale=rstd[:, 1:2]).then_inc(xn1_ready, 1)
            act.wait_ge(ld_gmix, 16)
            for b in (1, 3):
                act.wait_ge(hT_tr, b + 1)
                for c in (2 * b, 2 * b + 1):
                    nc.scalar.activation(hT[:, c, :], bank(b)[:, (c % 2) * T:(c % 2 + 1) * T], ACT.Copy,
                                         scale=g_mix[:, c:c + 1]).then_inc(hT_act, 1)
            act.wait_ge(lam_dot, 2)
            nc.scalar.activation(lam4[:, 2:4], lam4[:, 0:2], ACT.Exp).then_inc(lam_exp, 1)

            def wait_step(i):
                act.wait_ge(step_done, i + 1)

            def pair_banks(i, lo=0, hi=P):
                return ps[lo:hi, (i % 2) * 2 * W512:((i % 2) * 2 + 2) * W512]

            wait_step(QB)
            act.wait_ge(zeroed, 2)
            nc.scalar.activation(qbz[HD:P, 1::2, :], pair_banks(QB, HD, P).rearrange("p (c t) -> p c t", c=4), ACT.Copy,
                                 scale=Q_SCALE).then_inc(evac[QB], 1)
            wait_step(KB)
            nc.scalar.copy(r_kv[:, 0:1024], pair_banks(KB)).then_inc(evac[KB], 1)
            wait_step(VB)
            nc.scalar.copy(r_kv[:, 1024:2048], pair_banks(VB)).then_inc(evac[VB], 1)

            def softplus_part(g):
                act.wait_ge(sb_abs, 4 * (g + 1))
                own.step(nc.scalar.activation(sp[:, :, :], sp[:, :, :], ACT.Exp))
                own.settle()
                nc.scalar.activation(sp[:, :, :], sp[:, :, :], ACT.Ln, bias=1.0).then_inc(sb_ln, 1)

            def stick_exp(g):
                act.wait_ge(sb_arg, 4 * (g + 1))
                nc.scalar.activation(zb[:, :, :], zb[:, :, :], ACT.Exp).then_inc(sb_a, 1)

            def stick_out(g):
                act.wait_ge(sb_o, g + 1)
                act.wait_ge(bias_parts, 5)
                nc.scalar.copy(obT[:, 2 * g:2 * g + 2, :], bank(4).rearrange("p (c t) -> p c t", c=2)).then_inc(sb_ev, 1)

            softplus_part(0)
            wait_step(TRQ)
            act.wait_ge(zeroed, 3)
            nc.scalar.activation(qaz[HD:P, 1::2, :], pair_banks(TRQ, HD, P).rearrange("p (c t) -> p c t", c=4),
                                 ACT.Copy, scale=Q_SCALE).then_inc(evac[TRQ], 1)
            stick_exp(0)
            wait_step(VA)
            nc.scalar.copy(r_va[:, :], pair_banks(VA)).then_inc(evac[VA], 1)
            stick_out(0)
            wait_step(TRK)
            nc.scalar.copy(r_ka[:, 0:W512], pair_banks(TRK)[:, 0:W512]).then_inc(evac[TRK], 1)
            softplus_part(1)

            def sigmoid_of(i, dst, half):
                wait_step(i)
                nc.scalar.activation(dst[:, 4 * half:4 * half + 4, :], pair_banks(i).rearrange("p (c t) -> p c t", c=4),
                                     ACT.Sigmoid).then_inc(evac[i], 1)

            sigmoid_of(GA0, sga, 0)
            stick_exp(1)
            sigmoid_of(GA1, sga, 1)
            stick_out(1)
            for h in range(HEADS):
                act.wait_ge(da_nm, h + 1)
                nc.scalar.activation(pb[:, h, 0:P], pb[:, h, 0:P], ACT.Exp, bias=nmx[:, h, 0:1],
                                     accum_out=den[:, h, 0:1])
                nc.scalar.activation(pb[:, h, P:BLOCKS], pb[:, h, P:BLOCKS], ACT.Exp, bias=nmx[:, h, 1:2],
                                     accum_out=den[:, h, 1:2]).then_inc(da_e, 1)
            sigmoid_of(GB0, sgb, 0)
            sigmoid_of(GB1, sgb, 1)

            def head_squares(heads):
                act.wait_ge(da_o, heads[-1] + 1)
                for hd, a in ((hd, a) for hd in heads for a in range(NT)):
                    c0 = (hd % 2) * T + a * P
                    junk = 2 * (hd % 2) + a
                    last = nc.scalar.activation(r_tb[:, junk * P:(junk + 1) * P], bank(6 + hd // 2)[:, c0:c0 + P],
                                                ACT.Square,
                                                accum_out=ossq[:, 2 * hd + a:2 * hd + a + 1])
                last.then_inc(da_ssq, 1)

            act.wait_ge(ld_bias3, 16 * 12)
            for hd in range(DA_HEADS):
                act.wait_ge(da_t, hd + 1)
                if hd >= 2:
                    act.wait_ge(da_o, hd - 1)
                nc.scalar.copy(wT[:, hd % 2, :], bank(4 + hd % 2)[:, 0:BLOCKS]).then_inc(da_wt, 1)
            head_squares((0, 1))
            act.wait_ge(da_ssq, 1)
            head_squares((2, 3))
            act.wait_ge(da_var, 1)
            nc.scalar.activation(ossq, ossq, ACT.Sqrt).then_inc(da_std, 1)
            act.wait_ge(tro, 1)
            nc.scalar.activation(oT[:, 0:2, :], bank(4).rearrange("p (c t) -> p c t", c=2), ACT.Copy,
                                 scale=g_sub8).then_inc(oT_act, 1)

            for a in range(NT):
                act.wait_ge(x1, a + 1)
                nc.scalar.activation(r_va[:, :], x3[:, a, :], ACT.Square,
                                     accum_out=ssq[:, a:a + 1]).then_inc(ssq2_ready, 1)
                act.wait_ge(ms2_ready, a + 1)
                nc.scalar.activation(std[:, a:a + 1], var[:, a:a + 1], ACT.Sqrt).then_inc(std2_ready, 1)
                act.wait_ge(tx_done, 2 * a + 2)
                act.wait_ge(ld_router, 16 * 3)
                for c in range(4, KC):
                    last = nc.scalar.activation(hTr[a][:, c, :],
                                                bank(5 + 2 * a)[:, (c % 4) * P:(c % 4 + 1) * P], ACT.Copy,
                                                scale=g_ffn[:, c:c + 1])
                last.then_inc(hTr_act, 1)
                act.wait_ge(rt_done, a + 1)
                nc.scalar.copy(lT[0:E, a * P:(a + 1) * P], bank(4 * a)[0:E, 0:P]).then_inc(lT_ready, 1)
                act.wait_ge(h_full, a + 1)
                nc.scalar.copy(h3[:, a, 0], h32[a]).then_inc(h_p1, 1)
                act.wait_ge(h_r1, a + 1)
                nc.scalar.copy(h3[:, a, 1], h32[a]).then_inc(h_p2, 1)
                act.wait_ge(neg_top, a + 1)
                nc.scalar.activation(ex[:, a, :], lg[:, a, :], ACT.Exp, bias=rt[:, 4 + a:5 + a]).then_inc(ex_ready, 1)

            def gathered(n_value):
                act.wait_ge(gat_done, n_value)
                for b in range(2):
                    nc.scalar.copy(xT[:, 4 * b:4 * b + 4, :],
                                   bank(T_B + b).rearrange("p (c s) -> p c s", c=4)).then_inc(xT_ready, 1)

            gathered(1)

            def expert_iteration(i, it):
                for q in range(PAIRS_PER_ITER):
                    n = it * PAIRS_PER_ITER + q
                    act.wait_ge(g_clipped, n + 1)
                    nc.scalar.activation(sg_s, g_s, ACT.Sigmoid, scale=ALPHA).then_inc(sig_ready, 1)
                    gathered(n + 2)
                    act.wait_ge(gt_done, n + 1)
                    nc.scalar.copy(g_T, bank(O_B)[:, 0:T]).then_inc(gt_ready, 1)
                    for b in range(2):
                        act.wait_ge(ht_done, n * 2 + b + 1)
                        nc.scalar.copy(hTm[:, 4 * b:4 * b + 4, :],
                                       bank(T_B + b).rearrange("p (c s) -> p c s", c=4)).then_inc(hT_ready, 1)
                    for b in range(2):
                        if b == 0:
                            act.wait_ge(down_done, n + 1)
                        else:
                            act.wait_ge(load_used, it * LOADS_PER_ITER + LOADS_PER_PAIR * (q + 1))
                        nc.scalar.copy(o_s[:, b * W512:(b + 1) * W512], bank(O_B + b)).then_inc(o_ready, 1)

            with act.Fori(0, ITERS) as i:
                expert_iteration(i, i)
            rounds = rounds_after_first(act, expert_iteration)
            act.wait_ge(y_added, rounds * (4 * PAIRS) + 1)
            nc.scalar.activation(r_va[:, :], x3[:, 1, :], ACT.Square, accum_out=ssq[:, 1:2]).then_inc(ssq1_ready, 1)
            act.wait_ge(fin_ms, 1)
            nc.scalar.activation(std, var, ACT.Sqrt).then_inc(fin_std, 1)

        @block.vector
        def _(dve):
            own = Steps(dve, dve_own)

            def square_sum(junk, a):
                return nc.vector.tensor_tensor_reduce(out=junk, in0=x3[:, a, :], in1=x3[:, a, :], scale=1.0, scalar=0.0,
                                                      op0=ALU.mult, op1=ALU.add, accum_out=ssq[:, a:a + 1])

            dve.wait_ge(ld_x[0], 16)
            own.step(square_sum(r_a1[:, 0:D], 0))
            own.settle()
            dve.wait_ge(ssq1_ready, 1)
            nc.vector.tensor_scalar(var, ssq, 1.0 / D, NORM_EPS, ALU.mult, ALU.add).then_inc(ms_ready, 1)
            dve.wait_ge(std_ready, 1)
            nc.vector.reciprocal(rstd, std).then_inc(rstd_ready, 1)
            dve.wait_ge(rstd_ready, 1)
            nc.vector.tensor_scalar(xn3[:, 0, :], x3[:, 0, :], rstd[:, 0:1], None, ALU.mult).then_inc(xn_ready, 1)
            dve.wait_ge(ld_gmix, 16)
            for b in (0, 2):
                dve.wait_ge(hT_tr, b + 1)
                for c in (2 * b, 2 * b + 1):
                    nc.vector.tensor_scalar(hT[:, c, :], bank(b)[:, (c % 2) * T:(c % 2 + 1) * T], g_mix[:, c:c + 1],
                                            None, ALU.mult).then_inc(hT_dve, 1)
            dve.wait_ge(ld_lam, 16 * 4)
            dve.wait_ge(ld_gsub, 16)
            for k in range(2):
                nc.vector.tensor_tensor_reduce(
                    out=r_w[:, 2048 + k * HD:2048 + (k + 1) * HD], in0=lam_in[:, 2 * k * HD:(2 * k + 1) * HD],
                    in1=lam_in[:, (2 * k + 1) * HD:(2 * k + 2) * HD], scale=1.0, scalar=0.0, op0=ALU.mult, op1=ALU.add,
                    accum_out=lam4[:, k:k + 1]).then_inc(lam_dot, 1)
            dve.wait_ge(lam_exp, 1)
            own.step(nc.vector.tensor_tensor(lamv[:, 0:1], lam4[:, 2:3], lam4[:, 3:4], ALU.subtract))
            own.step(nc.vector.tensor_scalar(g_sub8, g_sub[:, :], 1.0 - LAMBDA_INIT, None, ALU.mult))
            own.settle()
            own.step(nc.vector.tensor_scalar(lamv[:, 1:2], lamv[:, 0:1], LAMBDA_INIT, -1.0, ALU.add, ALU.mult))
            own.settle()

            def wait_step(i):
                dve.wait_ge(step_done, i + 1)

            def pair_banks(i, lo=0, hi=P):
                return ps[lo:hi, (i % 2) * 2 * W512:((i % 2) * 2 + 2) * W512]

            wait_step(QB)
            dve.wait_ge(zeroed, 2)
            nc.vector.tensor_scalar(qbz[0:HD, 0::2, :], pair_banks(QB, 0, HD).rearrange("p (c t) -> p c t", c=4),
                                    Q_SCALE, None, ALU.mult).then_inc(evac[QB], 1)
            dve.wait_ge(ld_const, 16 * 2)
            dve.wait_ge(const_cast, 1)

            def stick_scores(g):
                if g:
                    dve.wait_ge(sb_o, g)
                for hh in range(4):
                    dve.wait_ge(sb_z, 4 * g + hh + 1)
                    z = bank(4 + hh)[:, 0:BLOCKS].rearrange("p (b n) -> p b n", b=3)
                    o = zb[:, hh, :].rearrange("p (b n) -> p b n", b=3)
                    own.step(nc.vector.tensor_tensor(o[:, 0::2, :], z[:, 0::2, :],
                                                     mask_sb.unsqueeze(1).to_broadcast([P, 2, P]), ALU.add))
                    own.step(nc.vector.tensor_copy(o[:, 1, :], z[:, 1, :]))
                    own.settle()
                    nc.vector.scalar_tensor_tensor(out=sp[:, hh, :], in0=zb[:, hh, :], scalar=-1.0, in1=zb[:, hh, :],
                                                   op0=ALU.mult, op1=ALU.min).then_inc(sb_abs, 1)

            def stick_softplus(g):
                dve.wait_ge(sb_ln, g + 1)
                nc.vector.scalar_tensor_tensor(out=r_w[:, 4 * BLOCKS:8 * BLOCKS], in0=r_w[:, 0:4 * BLOCKS], scalar=0.0,
                                               in1=r_w[:, 4 * BLOCKS:8 * BLOCKS], op0=ALU.max,
                                               op1=ALU.add).then_inc(sb_sp, 1)

            def stick_argument(g):
                for hh in range(4):
                    dve.wait_ge(sb_r, 4 * g + hh + 1)
                    nc.vector.tensor_tensor(zb[:, hh, :], bank(4 + hh)[:, 0:BLOCKS], zb[:, hh, :],
                                            ALU.add).then_inc(sb_arg, 1)

            def rotate(i):
                wait_step(i)
                if i == KA:
                    dve.wait_ge(step_done, TRQ + 1)
                xs = pair_banks(i).rearrange("p (a h w d) -> p a h w d", a=NT, h=HEADS, w=2)
                tb = r_tb[:, :].rearrange("p (h w d) -> p h w d", h=HEADS, w=2)
                for a in range(NT):
                    cos, sin, nsin = (rope[:, a, w, :] for w in range(3))
                    ra = rot[:, a, :]
                    own.settle()
                    nc.vector.tensor_tensor(ra.rearrange("p (m d) -> p m d", d=HD // 2),
                                            xs[:, a].rearrange("p h w d -> p (h w) d"),
                                            cos.unsqueeze(1).to_broadcast([P, 2 * HEADS, HD // 2]), ALU.mult)
                    nc.vector.tensor_tensor(tb[:, :, 0, :], xs[:, a, :, 1, :],
                                            nsin.unsqueeze(1).to_broadcast([P, HEADS, HD // 2]), ALU.mult)
                    last = nc.vector.tensor_tensor(tb[:, :, 1, :], xs[:, a, :, 0, :],
                                                   sin.unsqueeze(1).to_broadcast([P, HEADS, HD // 2]), ALU.mult)
                    own.step(last)
                    own.settle()
                    add = nc.vector.tensor_tensor(ra, ra, r_tb[:, :], ALU.add)
                    if a == NT - 1:
                        add.then_inc(rope_done, 1)
                        nc.vector.engine_nop().then_inc(evac[i], 1)
                    else:
                        own.step(add)

            stick_scores(0)
            stick_softplus(0)
            dve.wait_ge(zeroed, 3)
            dve.wait_ge(ld_bias3, 16 * 12)
            rotate(QA)
            rotate(KA)
            nc.vector.tensor_scalar(qaz[0:HD, 0::2, :], pair_banks(TRQ, 0, HD).rearrange("p (c t) -> p c t", c=4),
                                    Q_SCALE, None, ALU.mult).then_inc(evac[TRQ], 1)
            stick_argument(0)
            wait_step(TRK)
            nc.vector.tensor_copy(r_ka[:, W512:2 * W512], pair_banks(TRK)[:, W512:2 * W512]).then_inc(evac[TRK], 1)
            stick_scores(1)
            stick_softplus(1)
            stick_argument(1)

            dve.wait_ge(sb_o, 2)
            for h in range(HEADS):
                dve.wait_ge(da_s, h + 1)
                s = bank(4 + h % 4)
                own.step(nc.vector.tensor_tensor_reduce(
                    out=pb[:, h, 0:P], in0=s[:, 0:P], in1=mask_da[:, P:2 * P], scale=1.0, scalar=-3e38, op0=ALU.add,
                    op1=ALU.max, accum_out=mx[:, h, 0:1]))
                nc.vector.tensor_tensor_reduce(
                    out=pb[:, h, P:BLOCKS], in0=s[:, P:BLOCKS], in1=mask_da, scale=1.0, scalar=-3e38, op0=ALU.add,
                    op1=ALU.max, accum_out=mx[:, h, 1:2]).then_inc(da_read, 1)
                own.settle()
                dve.wait_ge(da_read, h + 1)
                nc.vector.tensor_scalar(nmx[:, h, :], mx[:, h, :], -1.0, None, ALU.mult).then_inc(da_nm, 1)
            for hd in range(DA_HEADS):
                h1, h2 = 2 * hd, 2 * hd + 1
                dve.wait_ge(da_e, h2 + 1)
                own.step(nc.vector.reciprocal(rden[:, h1:h2 + 1, :], den[:, h1:h2 + 1, :]))
                own.settle()
                own.step(nc.vector.tensor_scalar(c2[:, hd, :], rden[:, h2, :], lamv[:, 1:2], None, ALU.mult))
                own.settle()
                spans = ((0, P), (P, BLOCKS))
                for a, (lo, hi) in enumerate(spans):
                    own.step(nc.vector.tensor_scalar(pb[:, h2, lo:hi], pb[:, h2, lo:hi], c2[:, hd, a:a + 1], None,
                                                     ALU.mult))
                own.settle()
                for a, (lo, hi) in enumerate(spans):
                    last = nc.vector.scalar_tensor_tensor(out=pb[:, h1, lo:hi], in0=pb[:, h1, lo:hi],
                                                          scalar=rden[:, h1, a:a + 1], in1=pb[:, h2, lo:hi],
                                                          op0=ALU.mult, op1=ALU.add)
                last.then_inc(da_w, 1)
            dve.wait_ge(da_ssq, 2)
            nc.vector.tensor_scalar(ossq, ossq, 1.0 / P, NORM_EPS, ALU.mult, ALU.add).then_inc(da_var, 1)
            dve.wait_ge(da_std, 1)
            own.step(nc.vector.reciprocal(orstd, ossq))
            own.settle()
            for hd in range(DA_HEADS):
                for a in range(NT):
                    c0 = (hd % 2) * T + a * P
                    last = nc.vector.tensor_scalar(on3[:, a, hd * P:(hd + 1) * P], bank(6 + hd // 2)[:, c0:c0 + P],
                                                   orstd[:, 2 * hd + a:2 * hd + a + 1], None, ALU.mult)
            last.then_inc(on_ready, 1)
            dve.wait_ge(tro, 1)
            nc.vector.tensor_scalar(oT[:, 2:4, :], bank(5).rearrange("p (c t) -> p c t", c=2), g_sub8, None,
                                    ALU.mult).then_inc(oT_dve, 1)
            dve.wait_ge(evac[GB1], 1)
            for b in range(4):
                dve.wait_ge(yb_done, b + 1)
                own.step(nc.vector.tensor_tensor(r_qa[:, b * W512:(b + 1) * W512], bank(b),
                                                 r_qa[:, b * W512:(b + 1) * W512], ALU.mult))
            for b in range(4):
                dve.wait_ge(ya_done, b + 1)
                cols = slice(b * W512, (b + 1) * W512)
                own.step(nc.vector.tensor_tensor(r_a1[:, cols], bank(4 + b), r_a2[:, cols], ALU.mult))
                own.settle()
                nc.vector.tensor_tensor(r_a1[:, cols], r_a1[:, cols], r_qa[:, cols], ALU.add).then_inc(mix_ready, 1)
            for a in range(NT):
                dve.wait_ge(wo_done, a + 1)
                for half in range(2):
                    cols = slice(half * W512, (half + 1) * W512)
                    last = nc.vector.tensor_tensor(x3[:, a, cols], bank(2 * a + half), x3[:, a, cols], ALU.add)
                last.then_inc(x1, 1)
                dve.wait_ge(ssq2_ready, a + 1)
                nc.vector.tensor_scalar(var[:, a:a + 1], ssq[:, a:a + 1], 1.0 / D, NORM_EPS, ALU.mult,
                                        ALU.add).then_inc(ms2_ready, 1)
                dve.wait_ge(std2_ready, a + 1)
                own.step(nc.vector.reciprocal(rstd[:, a:a + 1], std[:, a:a + 1]))
                dve.wait_ge(tx_done, 2 * a + 1)
                dve.wait_ge(ld_router, 16 * 3)
                nc.vector.tensor_tensor(hTr[a][:, 0:4, :],
                                        bank(4 + 2 * a).rearrange("p (c t) -> p c t", c=4),
                                        g_ffn[:, 0:4].unsqueeze(2).to_broadcast([P, 4, P]), ALU.mult).then_inc(hTr_dve, 1)
                own.settle()
                dve.wait_ge(ld_gB, 16)
                if a == 0:
                    dve.wait_ge(rt_done, 1)
                nc.vector.scalar_tensor_tensor(
                    out=h32[a], in0=x3[:, a, :].rearrange("p (m c) -> p c m", c=KC), scalar=rstd[:, a:a + 1],
                    in1=gB.rearrange("p (m c) -> p c m", c=KC), op0=ALU.mult, op1=ALU.mult).then_inc(h_full, 1)
                dve.wait_ge(h_p1, a + 1)
                nc.vector.tensor_tensor(h32[a], h32[a], h3[:, a, 0], ALU.subtract).then_inc(h_r1, 1)
                dve.wait_ge(rt_tr, a + 1)
                own.step(nc.vector.scalar_tensor_tensor(out=lg[:, a, :], in0=bank(1 + 4 * a)[:, 0:E],
                                                        scalar=rstd[:, a:a + 1], in1=br[:, :], op0=ALU.mult,
                                                        op1=ALU.add))
                own.settle()
                own.step(nc.vector.max(top8[:, a, :], lg[:, a, :]))
                own.settle()
                nc.vector.tensor_scalar(rt[:, 4 + a:5 + a], top8[:, a, 0:1], -1.0, None, ALU.mult).then_inc(neg_top, 1)
                fourth = top8[:, a, TOP_K - 1:TOP_K]
                own.step(nc.vector.tensor_scalar(gt[:, a, :], lg[:, a, :], fourth, 0.0, ALU.is_gt, ALU.add,
                                                 accum_out=rt[:, a:a + 1]))
                own.step(nc.vector.tensor_scalar(eq[:, a, :], lg[:, a, :], fourth, None, ALU.is_equal))
                own.settle()
                own.step(nc.vector.tensor_scalar(rt[:, 2 + a:3 + a], rt[:, a:a + 1], -1.0, TOP_K + 0.5, ALU.mult,
                                                 ALU.add))
                own.step(nc.vector.tensor_tensor_scan(cum[:, a, :], ones_row, eq[:, a, :], 0.0, ALU.mult, ALU.add))
                own.settle()
                own.step(nc.vector.scalar_tensor_tensor(out=eq[:, a, :], in0=cum[:, a, :], scalar=rt[:, 2 + a:3 + a],
                                                        in1=eq[:, a, :], op0=ALU.is_lt, op1=ALU.mult))
                own.settle()
                own.step(nc.vector.tensor_tensor(mask[:, a, :], eq[:, a, :], gt[:, a, :], ALU.add))
                own.settle()
                nc.vector.tensor_copy(mask_b[:, a, :], mask[:, a, :]).then_inc(mask_ready, 1)
                dve.wait_ge(h_p2, a + 1)
                dve.wait_ge(h_r1, a + 1)
                nc.vector.tensor_tensor(h3[:, a, 2], h32[a], h3[:, a, 1], ALU.subtract).then_inc(h_ready, 1)
                dve.wait_ge(ex_ready, a + 1)
                own.step(nc.vector.tensor_tensor_reduce(out=ex[:, a, :], in0=ex[:, a, :], in1=mask[:, a, :], scale=1.0,
                                                        scalar=0.0, op0=ALU.mult, op1=ALU.add,
                                                        accum_out=rt[:, 6 + a:7 + a]))
                if a == NT - 1:
                    dve.wait_ge(rk_done, 1)
                    own.step(nc.vector.scalar_tensor_tensor(
                        out=rk1, in0=bank(2)[:, 0:2 * E].rearrange("p (a e) -> p a e", a=NT), scalar=1.0, in1=mask,
                        op0=ALU.add, op1=ALU.mult))
                    own.settle()
                    own.step(nc.vector.tensor_scalar(rkx[:, :, 0:E], rk1, -1.0, None, ALU.add))
                own.settle()
                own.step(nc.vector.reciprocal(rt[:, 8 + a:9 + a], rt[:, 6 + a:7 + a]))
                if a == 0:
                    own.settle()
                    own.step(nc.vector.tensor_scalar(gates[:, a, :], ex[:, a, :], rt[:, 8 + a:9 + a], None, ALU.mult))

            def select(q, n):
                for k in range(2):
                    for a in range(NT):
                        nc.vector.tensor_scalar(s_sel[:, a, k * SLOTS:(k + 1) * SLOTS], iota,
                                                rkx[:, a, bass.ds(n * 2 + k, 1)], None, ALU.is_equal)
                    last = nc.vector.tensor_copy(oh[q][0:3 * E, k * SLOTS:(k + 1) * SLOTS],
                                                 e3_b[0:3 * E, bass.ds(n * 2 + k, 1)].to_broadcast([3 * E, SLOTS]))
                last.then_inc(sel_ready, 1)

            select(0, 0)
            own.settle()
            own.step(nc.vector.tensor_scalar(gates[:, 1, :], ex[:, 1, :], rt[:, 9:10], None, ALU.mult))
            own.step(nc.vector.reduce_max(rt[:, 10:11], bank(2)[:, 2 * E:3 * E], AX.X))
            own.step(nc.vector.memset(rkx[:, :, ROUNDS * E:N_ROUND_COLS], -1.0))
            own.step(nc.vector.memset(gx[:, :, ROUNDS * E:N_ROUND_COLS], 0.0))
            own.settle()
            for r in range(ROUNDS):
                if r:
                    own.step(nc.vector.tensor_scalar(rkx[:, :, r * E:(r + 1) * E], rk1, -1.0 - SLOTS * r, None, ALU.add))
                own.step(nc.vector.tensor_copy(gx[:, :, r * E:(r + 1) * E], gates))
            for r in range(ROUNDS):
                own.step(nc.vector.tensor_scalar(nrd[:, r:r + 1], rt[:, 10:11], float(SLOTS * r) if r else -1.0, None,
                                                 ALU.is_gt))
            own.settle()
            own.step(nc.vector.tensor_reduce(rt[:, 11:12], nrd, AX.X, ALU.add))
            own.settle()
            nc.vector.tensor_copy(nr_i[:, :], rt[:, 11:12]).then_inc(nr_ready, 1)
            dve.wait_ge(x1, NT)
            nc.vector.engine_nop().then_inc(y_added, 1)
            base = own.n

            def expert_iteration(i, it):
                steps = Steps(dve, dve_own, it * DVE_STEPS_PER_ITER + base)
                for q in range(PAIRS_PER_ITER):
                    n = it * PAIRS_PER_ITER + q
                    dve.wait_ge(load_used, it * LOADS_PER_ITER + LOADS_PER_PAIR * q + 4)
                    nc.vector.tensor_scalar(g_s, bank(G_B, 2), LIMIT, None, ALU.min).then_inc(g_clipped, 1)
                    for k in range(2):
                        for a in range(NT):
                            last = nc.vector.tensor_scalar(gs[:, a, k * SLOTS:(k + 1) * SLOTS], iota,
                                                           rkx[:, a, bass.ds(n * 2 + k, 1)],
                                                           gx[:, a, bass.ds(n * 2 + k, 1)], ALU.is_equal, ALU.mult)
                    last.then_inc(gs_ready, 1)
                    select((q + 1) % 2, n + 1)
                    dve.wait_ge(load_used, it * LOADS_PER_ITER + LOADS_PER_PAIR * q + 8)
                    steps.step(nc.vector.tensor_scalar(u_s, bank(U_B, 2), LIMIT, -LIMIT, ALU.min, ALU.max))
                    dve.wait_ge(sig_ready, n + 1)
                    steps.step(nc.vector.tensor_tensor(g_s, g_s, sg_s, ALU.mult))
                    steps.settle()
                    nc.vector.scalar_tensor_tensor(out=g_s, in0=u_s, scalar=1.0, in1=g_s, op0=ALU.add,
                                                   op1=ALU.mult).then_inc(act_ready, 1)
                    dve.wait_ge(y_added, n * 4 + 1)
                    for half, b in ((0, U_B), (1, T_B)):
                        dve.wait_ge(sc_done, n * 2 + half + 1)
                        for a in range(NT):
                            cols = slice(half * W512, (half + 1) * W512)
                            nc.vector.tensor_tensor(x3[:, a, cols], bank(b + a), x3[:, a, cols],
                                                    ALU.add).then_inc(y_added, 1)
                assert steps.n == DVE_STEPS_PER_ITER

            with dve.Fori(0, ITERS) as i:
                expert_iteration(i, i)
            rounds = rounds_after_first(dve, expert_iteration)

            dve.wait_ge(y_added, rounds * (4 * PAIRS) + 1)
            square_sum(r_a1[:, 0:D], 0).then_inc(rstd_ready, 1)
            dve.wait_ge(rstd_ready, 2)
            dve.wait_ge(ssq1_ready, 2)
            nc.vector.tensor_scalar(var, ssq, 1.0 / D, NORM_EPS, ALU.mult, ALU.add).then_inc(fin_ms, 1)
            dve.wait_ge(fin_std, 1)
            nc.vector.reciprocal(rstd, std).then_inc(rstd_ready, 1)
            dve.wait_ge(rstd_ready, 3)
            dve.wait_ge(ld_gfin, 16)
            for a in range(NT):
                nc.vector.scalar_tensor_tensor(out=x3[:, a, :], in0=x3[:, a, :], scalar=rstd[:, a:a + 1], in1=gfin,
                                               op0=ALU.mult, op1=ALU.mult).then_inc(fin_done, 1)

        @block.tensor
        def _(pe):
            mm = nc.tensor.matmul

            def wait_slot(n):
                pe.wait_ge(slot_loaded[n % RING], 16 * (n // RING + 1))

            pe.wait_ge(ld_id, 16)
            pe.wait_ge(xn_ready, 1)
            pe.wait_ge(xn1_ready, 1)
            for c in range(KC):
                for a in range(NT):
                    last = nc.tensor.transpose(bank(c // 2)[:, (c % 2) * T + a * P:(c % 2) * T + (a + 1) * P],
                                               xn3[:, a, c:D:KC], ident)
                if c % 2:
                    last.then_inc(hT_tr, 1)
            pe.wait_ge(hT_dve, KC // 2)
            pe.wait_ge(hT_act, KC // 2)

            def project(i):
                n = STEP_SLOT[i]
                wait_slot(n)
                if i >= 2:
                    pe.wait_ge(evac[i - 2], EVACUATIONS[i - 2])
                w = slot(n % RING, KC, W512)
                b = (i % 2) * 2
                if i in (VB, QA, KA, VA):
                    for a in range(NT):
                        for c in range(KC):
                            last = mm(bank(b + a), hT[:, c, a * P:(a + 1) * P], w[:, c, :], start=c == 0, stop=c == KC - 1)
                else:
                    for j in range(4):
                        for c in range(KC):
                            last = mm(bank(b + j // 2)[:, (j % 2) * T:(j % 2 + 1) * T], w[:, c, j * P:(j + 1) * P],
                                      hT[:, c, :], start=c == 0, stop=c == KC - 1)
                last.then_inc(step_done, 1)

            def transpose_heads(i, rotated):
                pe.wait_ge(rope_done, rotated)
                pe.wait_ge(evac[i - 2], EVACUATIONS[i - 2])
                for j in range(4):
                    for a in range(NT):
                        c0 = (i % 2) * 2 * W512 + j * T + a * P
                        last = nc.tensor.transpose(ps[:, c0:c0 + P], rot[:, a, j * P:(j + 1) * P], ident)
                last.then_inc(step_done, 1)

            def stick_scores(g):
                for hh in range(4):
                    h = 4 * g + hh
                    mm(bank(4 + hh)[:, 0:T], kbT[:, h // 2, 0:P], qbz[:, h, :], start=True, stop=True)
                    mm(bank(4 + hh)[:, T:BLOCKS], kbT[:, h // 2, P:T], qbz[:, h, P:T], start=True,
                       stop=True).then_inc(sb_z, 1)

            def stick_sums(g):
                pe.wait_ge(sb_sp, g + 1)
                for hh in range(4):
                    b = bank(4 + hh)
                    mm(b[:, 0:BLOCKS], tri_neg, sp[:, hh, :], start=True, stop=False)
                    mm(b[:, P:T], one_neg, sp[:, hh, T:BLOCKS], start=False, stop=True).then_inc(sb_r, 1)

            def stick_values(g):
                pe.wait_ge(sb_a, g + 1)
                for hh in range(4):
                    h = 4 * g + hh
                    lo = (hh % 2) * HD
                    o = bank(4)[lo:lo + HD, (hh // 2) * T:(hh // 2 + 1) * T]
                    mm(o, vb3[:, 0, h * HD:(h + 1) * HD], zb[:, hh, 0:T], start=True, stop=False)
                    last = mm(o[:, P:T], vb3[:, 1, h * HD:(h + 1) * HD], zb[:, hh, T:BLOCKS], start=False, stop=True)
                last.then_inc(sb_o, 1)

            project(QB)
            project(KB)
            project(VB)
            pe.wait_ge(evac[KB], 1)
            stick_scores(0)
            project(QA)
            project(KA)
            transpose_heads(TRQ, 1)
            stick_sums(0)
            project(VA)
            stick_values(0)
            transpose_heads(TRK, 2)
            pe.wait_ge(sb_ev, 1)
            stick_scores(1)
            project(GA0)
            stick_sums(1)
            project(GA1)
            stick_values(1)
            pe.wait_ge(evac[TRQ], 2)
            pe.wait_ge(evac[TRK], 2)
            pe.wait_ge(sb_ev, 2)
            for h in range(HEADS):
                if h >= 4:
                    pe.wait_ge(da_read, h - 3)
                s = bank(4 + h % 4)
                mm(s[:, 0:P], qaz[:, h, 0:P], kaT[:, h // 2, 0:P], start=True, stop=True)
                mm(s[:, P:BLOCKS], qaz[:, h, P:T], kaT[:, h // 2, :], start=True, stop=True).then_inc(da_s, 1)
            project(GB0)
            project(GB1)

            def transpose_weights(hd):
                pe.wait_ge(da_w, hd + 1)
                if hd >= 2:
                    pe.wait_ge(da_wt, hd - 1)
                else:
                    pe.wait_ge(da_read, HEADS)
                for k in range(3):
                    last = nc.tensor.transpose(bank(4 + hd % 2)[:, k * P:(k + 1) * P], pb[:, 2 * hd, k * P:(k + 1) * P],
                                               ident)
                last.then_inc(da_t, 1)

            def head_values(hd):
                pe.wait_ge(da_wt, hd + 1)
                o = bank(6 + hd // 2)[:, (hd % 2) * T:(hd % 2 + 1) * T]
                w = wT[:, hd % 2, :]
                v = va3[:, :, hd * P:(hd + 1) * P]
                mm(o[:, 0:P], w[:, 0:P], v[:, 0], start=True, stop=True)
                mm(o[:, P:T], w[:, P:T], v[:, 0], start=True, stop=False)
                mm(o[:, P:T], w[:, T:BLOCKS], v[:, 1], start=False, stop=True).then_inc(da_o, 1)

            pe.wait_ge(evac[VA], 1)
            transpose_weights(0)
            transpose_weights(1)
            head_values(0)
            transpose_weights(2)
            head_values(1)
            transpose_weights(3)
            head_values(2)
            head_values(3)
            wait_slot(10)
            pe.wait_ge(evac[GB0], 1)
            pe.wait_ge(evac[GB1], 1)

            def project_out(n, first_bank, heads, done):
                w = slot(n % RING, 4, D)
                for j in range(KC):
                    for c in range(4):
                        last = mm(bank(first_bank + j // 2)[:, (j % 2) * T:(j % 2 + 1) * T], w[:, c, j * P:(j + 1) * P],
                                  heads[:, c, :], start=c == 0, stop=c == 3)
                    if j % 2:
                        last.then_inc(done, 1)

            project_out(10, 0, obT, yb_done)
            pe.wait_ge(on_ready, 1)
            for hd in range(DA_HEADS):
                for a in range(NT):
                    c0 = (hd % 2) * T + a * P
                    last = nc.tensor.transpose(bank(4 + hd // 2)[:, c0:c0 + P], on3[:, a, hd * P:(hd + 1) * P], ident)
            last.then_inc(tro, 1)
            wait_slot(11)
            pe.wait_ge(oT_act, 1)
            pe.wait_ge(oT_dve, 1)
            project_out(11, 4, oT, ya_done)
            wait_slot(12)
            wait_slot(13)

            def router_transposes(a):
                pe.wait_ge(x1, a + 1)
                for c in range(KC):
                    last = nc.tensor.transpose(bank(4 + 2 * a + c // 4)[:, (c % 4) * P:(c % 4 + 1) * P], x3[:, a, c:D:KC],
                                               ident)
                    if c % 4 == 3:
                        last.then_inc(tx_done, 1)

            def router_logits(a):
                pe.wait_ge(hTr_dve, a + 1)
                pe.wait_ge(hTr_act, a + 1)
                for c in range(KC):
                    last = mm(bank(4 * a)[0:E, 0:P], wr3[:, c, :], hTr[a][:, c, :], start=c == 0,
                              stop=c == KC - 1)
                last.then_inc(rt_done, 1)

            def router_back(a):
                pe.wait_ge(lT_ready, a + 1)
                nc.tensor.transpose(bank(1 + 4 * a)[:, 0:E], lT[0:E, a * P:(a + 1) * P], ident[0:E, 0:E]).then_inc(rt_tr, 1)

            for a in range(NT):
                for j in range(KC):
                    pe.wait_ge(mix_ready, j // 2 + 1)
                    w = slot((12 + j // 4) % RING, 4, D)
                    for half in range(2):
                        last = mm(bank(2 * a + half), mixT[:, j, a * P:(a + 1) * P],
                                  w[:, j % 4, half * W512:(half + 1) * W512], start=j == 0, stop=j == KC - 1)
                    if a == 1 and j == 1:
                        router_transposes(0)
                    if a == 1 and j == 4:
                        router_logits(0)
                    if a == 1 and j == 6:
                        router_back(0)
                last.then_inc(wo_done, 1)
            router_transposes(1)
            router_logits(1)
            r = bank(2)
            pe.wait_ge(mask_ready, 1)
            mm(r[:, 0:E], su_b[:, :], mask_b[:, 0, :], start=True, stop=True)
            router_back(1)
            pe.wait_ge(mask_ready, 2)
            mm(r[:, E:2 * E], one_b[:, :], mask_b[:, 0, :], start=True, stop=False)
            mm(r[:, E:2 * E], su_b[:, :], mask_b[:, 1, :], start=False, stop=True)
            mm(r[:, 2 * E:3 * E], one_b[:, :], mask_b[:, 0, :], start=True, stop=False)
            mm(r[:, 2 * E:3 * E], one_b[:, :], mask_b[:, 1, :], start=False, stop=True).then_inc(rk_done, 1)

            def gather(n_value):
                pe.wait_ge(sel_ready, n_value)
                for c in range(KC):
                    for k, (a, w) in enumerate((a, w) for a in range(NT) for w in range(3)):
                        last = mm(bank(T_B + c // 4)[:, (c % 4) * P:(c % 4 + 1) * P], h3[:, a, w, c, :],
                                  s_sel[:, a, :], start=k == 0, stop=k == 2 * 3 - 1)
                last.then_inc(gat_done, 1)

            pe.wait_ge(h_ready, 2)
            gather(1)
            pe.wait_ge(ld_bias3, 16 * 12)

            def expert_iteration(i, it):
                for q in range(PAIRS_PER_ITER):
                    n = it * PAIRS_PER_ITER + q

                    def loaded(m):
                        p = LOADS_PER_PAIR * q + m
                        b = SLOT_OF[p]
                        per_load = 16 if b <= RING else 2 * 16
                        before = len(range(b, HEAD_LOADS, RING)) if b < RING else 0
                        pe.wait_ge(slot_loaded[b], it * (per_load * SLOT_OF.count(b))
                                   + 16 * before + per_load * SLOT_OF[:p + 1].count(b))
                        return [expert_part(b, k).rearrange("p (c n) -> p c n", c=2) for k in range(2)]

                    def biases(which, banks):
                        for half in range(2):
                            mm(bank(banks + half), oh[q][0:3 * E, :], bias3[0:3 * E, which, half * W512:(half + 1) * W512],
                               start=True, stop=False, skip_group_check=True)

                    def gate_or_up(which, banks):
                        biases(which, banks)
                        for m in range(4):
                            w = loaded(4 * which + m)
                            for c in range(2):
                                for half in range(2):
                                    for k in range(2):
                                        rows = slice(k * SLOTS, (k + 1) * SLOTS)
                                        last = mm(bank(banks + half)[rows, :], xT[:, 2 * m + c, rows],
                                                  w[k][:, c, half * W512:(half + 1) * W512], start=False,
                                                  stop=m == 3 and c == 1, skip_group_check=True)
                            last.then_inc(load_used, 1)

                    pe.wait_ge(sel_ready, n + 1)
                    pe.wait_ge(xT_ready, n * 2 + 2)
                    gate_or_up(0, G_B)
                    pe.wait_ge(y_added, n * 4 + 1)
                    gate_or_up(1, U_B)
                    gather(n + 2)
                    pe.wait_ge(gs_ready, n + 1)
                    for a in range(NT):
                        last = nc.tensor.transpose(bank(O_B)[:, a * P:(a + 1) * P], gs[:, a, :], ident)
                    last.then_inc(gt_done, 1)
                    pe.wait_ge(xT_ready, n * 2 + 4)
                    pe.wait_ge(act_ready, n + 1)
                    for b in range(2):
                        for c in range(4):
                            last = nc.tensor.transpose(bank(T_B + b)[:, c * P:(c + 1) * P],
                                                       g_s[:, b * W512 + c:(b + 1) * W512:4], ident)
                        last.then_inc(ht_done, 1)
                    pe.wait_ge(gt_ready, n + 1)
                    biases(2, O_B)
                    for m in range(4):
                        w = loaded(8 + m)
                        pe.wait_ge(hT_ready, n * 2 + m // 2 + 1)
                        order = [(c, half) for c in range(2) for half in range(2)]
                        if m == 3:
                            order.sort(key=lambda x: x[1])
                        for c, half in order:
                            for k in range(2):
                                rows = slice(k * SLOTS, (k + 1) * SLOTS)
                                last = mm(bank(O_B + half)[rows, :], hTm[:, 2 * m + c, rows],
                                          w[k][:, c, half * W512:(half + 1) * W512], start=False,
                                          stop=m == 3 and c == 1, skip_group_check=True)
                            if m == 3 and c == 1 and half == 0:
                                last.then_inc(down_done, 1)
                        last.then_inc(load_used, 1)
                    pe.wait_ge(hT_ready, n * 2 + 2)
                    for half, b in ((0, U_B), (1, T_B)):
                        pe.wait_ge(o_ready, n * 2 + half + 1)
                        for a in range(NT):
                            last = mm(bank(b + a), g_T[:, a * P:(a + 1) * P], o_s[:, half * W512:(half + 1) * W512],
                                      start=True, stop=True)
                        last.then_inc(sc_done, 1)

            with pe.Fori(0, ITERS) as i:
                expert_iteration(i, i)
            rounds_after_first(pe, expert_iteration)


_INS = ["x", "norm_mix_g", "w_in", "lambda_q1", "lambda_k1", "lambda_q2", "lambda_k2", "da_subln_g", "w_da_out",
        "w_sb_out", "w_o", "norm_ffn_g", "w_router", "b_router", "w_gate", "b_gate", "w_up", "b_up", "w_down",
        "b_down", "norm_final_g"]
_SQUEEZED = {"x", "w_in", "w_da_out", "w_sb_out", "w_o", "w_router", "w_gate", "b_gate", "w_up", "b_up", "w_down",
             "b_down"}


def kernel(**inputs):
    import concourse.bacc as bacc
    from concourse.bass_utils import run_bass_kernel_spmd

    nc = bacc.Bacc("TRN2", target_bir_lowering=False, num_devices=1, dynamic_dma_scratch_size=1024)
    arrays, args = {}, []
    for name in _INS:
        a = np.ascontiguousarray(inputs[name])
        if name in _SQUEEZED:
            a = a.reshape(a.shape[1:])
        arrays[f"in_{name}"] = a
        args.append(nc.dram_tensor(f"in_{name}", a.shape, mybir.dt.from_np(a.dtype), kind="ExternalInput").ap())
    arrays["in_const"] = constants()
    args.append(nc.dram_tensor("in_const", arrays["in_const"].shape, F32, kind="ExternalInput").ap())
    args.append(nc.dram_tensor("out", (T, D), F32, kind="ExternalOutput").ap())
    build(nc, *args)
    r = run_bass_kernel_spmd(nc, [arrays], core_ids=[0])
    return r.results[0]["out"].reshape(1, T, D)
```

```python
from contextlib import ExitStack

import numpy as np

import concourse.bass as bass
import concourse.mybir as mybir
from concourse.alu_op_type import AluOpType as ALU

F32 = mybir.dt.float32
BF16 = mybir.dt.bfloat16
I32 = mybir.dt.int32
ACT = mybir.ActivationFunctionType
AX = mybir.AxisListType

P = 128
T = 256
NT = T // P
D = 1024
KC = D // P
HD = 64
HEADS = 8
DA_HEADS = 4
W512 = 512
E = 32
FF = 1024
TOP_K = 4
SLOTS = T // 4
ROUNDS = T // SLOTS
PAIRS = E // 2
PAIRS_PER_ITER = 2
ITERS = PAIRS // PAIRS_PER_ITER
RING = 8
SLOT_COLS = 4096
HEAD_LOADS = 14
LOADS_PER_PAIR = 12
LOADS_PER_ITER = PAIRS_PER_ITER * LOADS_PER_PAIR
SLOTS_AT_ALL = RING + 3
ROWS2 = 2 * D
BQ = FF // (P // E)
NORM_EPS = 1e-5
LAMBDA_INIT = 0.2
LIMIT = 7.0
ALPHA = 1.702
Q_SCALE = HD ** -0.5
MASKED = -1e30
BLOCKS = 3 * P

C_ID, C_ROPE, C_IOTA, C_TRI, C_ONE, C_MDA, C_MSB, C_KEEP = 0, 128, 320, 384, 512, 640, 896, 1024
C_SU, C_ONEP, C_E3 = 1024, 1152, 1280
N_ROUND_COLS = ROUNDS * E + 2
C_END = C_E3 + N_ROUND_COLS


def constants():
    c = np.zeros((P, C_END), np.float32)
    i = np.arange(P)
    c[:, C_ID:C_ID + P] = np.eye(P)
    c[:, C_TRI:C_TRI + P] = -(i[:, None] >= i[None, :]).astype(np.float32)
    c[:, C_ONE:C_ONE + P] = -1.0
    c[:, C_MDA + P:C_MDA + 2 * P] = np.where(i[None, :] <= i[:, None], 0.0, MASKED)
    c[:, C_MSB:C_MSB + P] = np.where(i[:, None] < i[None, :], 0.0, MASKED)
    inv = (1.0 / (np.float32(10000.0) ** (np.arange(0, HD, 2, dtype=np.float32) / np.float32(HD)))).astype(np.float32)
    ang = np.arange(T, dtype=np.float32)[:, None] * inv[None, :]
    rope = np.stack([np.cos(ang), np.sin(ang), -np.sin(ang)], 1).reshape(NT, P, 3, HD // 2)
    c[:, C_ROPE:C_ROPE + 192] = rope.transpose(1, 0, 2, 3).reshape(P, 192)
    c[:, C_IOTA:C_IOTA + SLOTS] = 1.0 + np.arange(SLOTS)[None, :]
    c[:, C_SU:C_SU + P] = (i[:, None] < i[None, :])
    c[:, C_ONEP:C_ONEP + P] = 1.0
    c[:, C_E3:C_E3 + N_ROUND_COLS] = (i[:, None] % E == np.arange(N_ROUND_COLS)[None, :] % E)
    return c


class Steps:

    def __init__(self, engine, semaphore, base=0):
        self.engine, self.semaphore, self.base, self.n = engine, semaphore, base, 0

    def step(self, instruction):
        instruction.then_inc(self.semaphore, 1)
        self.n += 1

    def settle(self):
        self.engine.wait_ge(self.semaphore, self.base + self.n)


QB, KB, VB, QA, KA, TRQ, VA, TRK, GA0, GA1, GB0, GB1 = range(12)
STEP_OF_SLOT = [QB, KB, VB, QA, KA, VA, GA0, GA1, GB0, GB1]
STEP_SLOT = {QB: 0, KB: 1, VB: 2, QA: 3, KA: 4, VA: 5, GA0: 6, GA1: 7, GB0: 8, GB1: 9}
STEP_COLS = {QA: 0, KA: 512, VA: 1024, QB: 1536, KB: 2048, VB: 2560, GA0: 3072, GA1: 3584, GB0: 4096, GB1: 4608}
EVACUATIONS = {QB: 2, KB: 1, VB: 1, QA: 1, KA: 1, TRQ: 2, VA: 1, TRK: 2, GA0: 1, GA1: 1, GB0: 1, GB1: 1}
DVE_STEPS_PER_ITER = 4


def slot_plan():
    thrice = {p: (HEAD_LOADS + u[0]) % RING for u in ((3, 13, 21), (4, 14, 22)) for p in u}
    turns = [(HEAD_LOADS + k) % RING for k in range(8) if k not in thrice] + [RING, RING + 1, RING + 2]
    slot_of = []
    n_turned = 0
    for p in range(LOADS_PER_ITER):
        if p in thrice:
            slot_of.append(thrice[p])
        else:
            slot_of.append(turns[n_turned % len(turns)])
            n_turned += 1
    assert n_turned % len(turns) == 0
    before = []
    for p in range(LOADS_PER_ITER):
        q = p - 1
        while slot_of[q % LOADS_PER_ITER] != slot_of[p]:
            q -= 1
        before.append(q)
    return slot_of, before


SLOT_OF, USED_BEFORE = slot_plan()
DMAS_OF = [2 if b > RING or p % LOADS_PER_PAIR == LOADS_PER_PAIR - 1 else 1 for p, b in enumerate(SLOT_OF)]
FIRST_LOADS = [0, 1, 2, 3, 4, 5, SLOT_OF.index(RING), 6, 7, SLOT_OF.index(RING + 1), SLOT_OF.index(RING + 2)]


def build(nc, x_d, norm_mix_g, w_in, lam_q1, lam_k1, lam_q2, lam_k2, subln_g, w_da_out, w_sb_out, w_o,
          norm_ffn_g, w_router, b_router, w_gate, b_gate, w_up, b_up, w_down, b_down, norm_final_g, const_d, out_d):
    ctx = ExitStack()
    with ctx:
        def sb(name, cols, dt=F32):
            return ctx.enter_context(nc.sbuf_tensor(name, [P, cols], dt))

        def sem(name):
            return ctx.enter_context(nc.semaphore(name))

        ring = sb("ring", RING * SLOT_COLS)

        def slot(s, rows, cols):
            return ring[:, s * SLOT_COLS:(s + 1) * SLOT_COLS].rearrange("p (c n) -> p c n", c=rows)

        def expert_part(s, k):
            if s < RING:
                lo = s * SLOT_COLS + k * ROWS2
                return ring[:, lo:lo + ROWS2]
            if s == RING:
                return r_qk[:, k * ROWS2:(k + 1) * ROWS2]
            if s == RING + 1:
                return (r_a[:, D:D + ROWS2], r_kvc[:, 2 * D:2 * D + ROWS2])[k]
            return (r_kvc[:, 0:ROWS2], r_r[:, R_SLOT:R_SLOT + ROWS2])[k]

        x_t = sb("x", NT * D)
        r_a = sb("region_a", 4096)
        r_a1 = r_a[:, 0:2048]
        r_a2 = r_a[:, 2048:4096]
        r_kvc = sb("region_kvc", 1024 + 2048 + 640 + 512)
        gB = r_kvc[:, 0:1024]
        r_kv = r_kvc[:, 1024:3072]
        cst2 = r_kvc[:, 3072:3712]
        r_tb = r_kvc[:, 3712:4224]
        r_qk = sb("region_qk", SLOT_COLS)
        r_qa = r_qk[:, 0:2048]
        r_ka = r_qk[:, 2048:3072]
        r_va = sb("region_va", 1024)
        r_w = sb("region_w", 3072)
        r_r = sb("region_r", 2 * BLOCKS + 2 * 1024 + 4 * HD + KC * E + 192)
        r_wt = r_r[:, 0:768]
        r_o = r_r[:, 768:1792]
        r_ob = r_r[:, 1792:2816]
        lam_in = r_r[:, 2816:3072]
        wr = r_r[:, 3072:3328]
        rope_t = r_r[:, 3328:3520]
        R_SLOT = 3520 - ROWS2
        ident = sb("ident", P)[:, :]
        iota = sb("iota", SLOTS)[:, :]
        su_b = sb("su_b", P, BF16)
        one_b = sb("one_b", P, BF16)
        e3_b = sb("e3_b", N_ROUND_COLS, BF16)
        g_mix = sb("g_mix", KC)
        g_ffn = sb("g_ffn", KC)
        g_sub = sb("g_sub", 1)
        br = sb("br", E)
        g_rows = r_w[0:KC, 2304:2304 + P]
        bias3 = sb("bias3", 3 * D, BF16)[:, :].rearrange("p (w n) -> p w n", w=3)
        small = sb("small", 128)

        x3 = x_t[:, :].rearrange("p (a n) -> p a n", a=NT)
        xn3 = r_kv[:, :].rearrange("p (a n) -> p a n", a=NT)
        hT = r_a1[:, :].rearrange("p (c t) -> p c t", c=KC)
        mixT = hT
        h32 = [r[:, 0:D].rearrange("p (c m) -> p c m", c=KC) for r in (r_kv[:, D:2 * D], r_kv)]
        g_s = o_s = r_a1[:, 0:D]
        u_s = sg_s = r_va[:, :]
        qbz = r_a2[:, :].rearrange("p (h t) -> p h t", h=HEADS)
        sga = r_a2[:, :].rearrange("p (c t) -> p c t", c=KC)
        hTr = [r_a2[:, a * D:(a + 1) * D].rearrange("p (c t) -> p c t", c=KC) for a in range(NT)]
        xT = r_a2[:, D:2 * D].rearrange("p (c s) -> p c s", c=KC)
        kbT = r_kv[:, 0:1024].rearrange("p (c t) -> p c t", c=4)
        vb3 = r_kv[:, 1024:2048].rearrange("p (a n) -> p a n", a=NT)
        gfin = ring[:, SLOT_OF[16] * SLOT_COLS:SLOT_OF[16] * SLOT_COLS + D]
        assert 16 not in USED_BEFORE and SLOT_OF[16] < RING
        qaz = r_qa[:, :].rearrange("p (h t) -> p h t", h=HEADS)
        sgb = r_qa[:, :].rearrange("p (c t) -> p c t", c=KC)
        braw = r_ob[:, 0:3 * BQ].rearrange("p (w n) -> p w n", w=3)
        bpart = [r[:, lo:lo + 3 * BQ // 2].bitcast(BF16).rearrange("p (w n) -> p w n", w=3)
                 for r, lo in ((r_tb, 0), (r_wt, 0), (r_wt, 3 * BQ // 2))]
        kaT = r_ka[:, :].rearrange("p (c t) -> p c t", c=4)
        va3 = r_va[:, :].rearrange("p (a n) -> p a n", a=NT)
        hTm = r_va[:, :].rearrange("p (c s) -> p c s", c=KC)
        zb = r_w[:, 0:4 * BLOCKS].rearrange("p (h n) -> p h n", h=4)
        sp = r_w[:, 4 * BLOCKS:8 * BLOCKS].rearrange("p (h n) -> p h n", h=4)
        pb = r_w[:, :].rearrange("p (h n) -> p h n", h=HEADS)
        on3 = r_w[:, 0:1024].rearrange("p (a n) -> p a n", a=NT)
        h3 = r_w[:, :].bitcast(BF16).rearrange("p (a w c m) -> p a w c m", a=NT, w=3, c=KC)
        wT = r_wt[:, :].rearrange("p (h n) -> p h n", h=2)
        rot = r_o[:, :].rearrange("p (a n) -> p a n", a=NT)
        oT = r_o[:, :].rearrange("p (h t) -> p h t", h=DA_HEADS)
        obT = r_ob[:, :].rearrange("p (h t) -> p h t", h=4)
        tri_neg = cst2[:, C_TRI - C_TRI:C_ONE - C_TRI]
        one_neg = cst2[:, C_ONE - C_TRI:C_MDA - C_TRI]
        mask_da = cst2[:, C_MDA - C_TRI:C_MSB - C_TRI]
        mask_sb = cst2[:, C_MSB - C_TRI:C_KEEP - C_TRI]
        rope = rope_t.rearrange("p (a w d) -> p a w d", a=NT, w=3)
        wr3 = wr[:, :].rearrange("p (c e) -> p c e", c=KC)

        ssq, table_junk, std, rstd = (small[:, 2 * k:2 * k + 2] for k in range(4))
        lam4, lamv = small[:, 8:12], small[:, 12:14]
        g_sub8 = small[:, 14:15]
        mx = small[:, 16:32].rearrange("p (h a) -> p h a", a=2)
        nmx = small[:, 32:48].rearrange("p (h a) -> p h a", a=2)
        den = small[:, 48:64].rearrange("p (h a) -> p h a", a=2)
        rden = small[:, 64:80].rearrange("p (h a) -> p h a", a=2)
        c2 = small[:, 80:88].rearrange("p (h a) -> p h a", a=2)
        ossq, orstd = small[:, 88:96], small[:, 96:104]
        nrd = small[:, 104:108]
        eps = small[:, 108:109]
        ssq_half, root_bias = small[:, 109:110], small[:, 110:111]
        nr_i = sb("nr_i", 1, I32)

        def carve(region, start, cols):
            return region[:, start:start + cols]

        gx = carve(r_r, 0, 2 * N_ROUND_COLS).rearrange("p (a n) -> p a n", a=NT)
        rkx = carve(r_r, 264, 2 * N_ROUND_COLS).rearrange("p (a n) -> p a n", a=NT)
        s_sel = carve(r_r, 528, 128).bitcast(BF16).rearrange("p (a s) -> p a s", a=NT)
        gs = carve(r_r, 656, 256).rearrange("p (a s) -> p a s", a=NT)
        g_T = carve(r_r, 912, 256)
        oh = [carve(r_r, 1168 + 64 * q, 64).bitcast(BF16) for q in range(2)]
        lT = carve(r_r, R_SLOT, 256)
        lg, eq, gt, cum, mask, ex, gates = (
            carve(r_r, R_SLOT + 256 + 64 * k, 64).rearrange("p (a e) -> p a e", a=NT) for k in range(7))
        top8 = carve(r_r, R_SLOT + 704, 16).rearrange("p (a e) -> p a e", a=NT)
        mask_b = carve(r_r, R_SLOT + 720, 32).bitcast(BF16).rearrange("p (a e) -> p a e", a=NT)
        rt = carve(r_r, R_SLOT + 752, 16)
        ones_row = sb("ones_row", E)[:, :]

        ps = ctx.enter_context(nc.psum_tensor("ps", [P, 8 * W512], F32))

        def bank(b, n=1):
            return ps[:, b * W512:(b + n) * W512]

        G_B, U_B, O_B, T_B = 0, 2, 4, 6

        slot_loaded = [sem(f"slot_loaded{s}") for s in range(SLOTS_AT_ALL)]
        half_loaded = {SLOT_OF[p]: sem(f"half_loaded{p}") for p in range(LOADS_PER_PAIR - 1, LOADS_PER_ITER, LOADS_PER_PAIR)}
        load_used = sem("load_used")
        ld_x = [sem(f"ld_x{a}") for a in range(NT)]
        ld_id, ld_gmix, ld_const, ld_const2 = sem("ld_id"), sem("ld_gmix"), sem("ld_const"), sem("ld_const2")
        ld_lam, ld_gsub, ld_router = sem("ld_lam"), sem("ld_gsub"), sem("ld_router")
        ld_gB, ld_gfin, ld_bias, ld_bias3 = sem("ld_gB"), sem("ld_gfin"), sem("ld_bias"), sem("ld_bias3")
        ld_gffn, g_tr, g_cols = sem("ld_gffn"), sem("g_tr"), sem("g_cols")
        stored = sem("stored")
        const_cast, zeroed = sem("const_cast"), sem("zeroed")
        dve_own, act_own = sem("dve_own"), sem("act_own")
        std_ready, rstd_ready = sem("std_ready"), sem("rstd_ready")
        xn_ready, xn1_ready, hT_tr = sem("xn_ready"), sem("xn1_ready"), sem("hT_tr")
        hT_dve, hT_act = sem("hT_dve"), sem("hT_act")
        lam_dot, lam_exp = sem("lam_dot"), sem("lam_exp")
        step_done = sem("step_done")
        evac = [sem(f"evac{i}") for i in range(12)]
        rope_done = sem("rope_done")
        sb_z, sb_abs, sb_ln, sb_sp, sb_r = sem("sb_z"), sem("sb_abs"), sem("sb_ln"), sem("sb_sp"), sem("sb_r")
        sb_arg, sb_a, sb_o, sb_ev = sem("sb_arg"), sem("sb_a"), sem("sb_o"), sem("sb_ev")
        da_s, da_read, da_nm, da_e, da_w = sem("da_s"), sem("da_read"), sem("da_nm"), sem("da_e"), sem("da_w")
        da_t, da_wt, da_o, da_ssq = sem("da_t"), sem("da_wt"), sem("da_o"), sem("da_ssq")
        da_var, da_std, on_ready, tro, oT_act, oT_dve = (sem(n) for n in (
            "da_var", "da_std", "on_ready", "tro", "oT_act", "oT_dve"))
        yb_done, ya_done, mix_ready, wo_done, x1 = (sem(n) for n in ("yb_done", "ya_done", "mix_ready", "wo_done", "x1"))
        tx_done, hTr_dve, hTr_act, rt_done, lT_ready, rt_tr = (sem(n) for n in (
            "tx_done", "hTr_dve", "hTr_act", "rt_done", "lT_ready", "rt_tr"))
        std2_ready, neg_top, bias_ready, ex_ready, mask_ready, rk_done = (sem(n) for n in (
            "std2_ready", "neg_top", "bias_ready", "ex_ready", "mask_ready", "rk_done"))
        h_full, h_p1, h_r1, h_p2, h_ready = (sem(n) for n in ("h_full", "h_p1", "h_r1", "h_p2", "h_ready"))
        bias_parts, nr_ready, ssq0_ready, ssq1_ready, ssq2_ready = (sem(n) for n in (
            "bias_parts", "nr_ready", "ssq0_ready", "ssq1_ready", "ssq2_ready"))
        sel_ready, gat_done, xT_ready, gate_done, up_done = (sem(n) for n in (
            "sel_ready", "gat_done", "xT_ready", "gate_done", "up_done"))
        g_clipped, gs_ready, gt_done, gt_ready, sig_ready, act_ready = (sem(n) for n in (
            "g_clipped", "gs_ready", "gt_done", "gt_ready", "sig_ready", "act_ready"))
        ht_done, hT_ready, down_done, o_ready, sc_done, y_added = (sem(n) for n in (
            "ht_done", "hT_ready", "down_done", "o_ready", "sc_done", "y_added"))
        fin_std, fin_done = sem("fin_std"), sem("fin_done")

        wg_v = w_gate.rearrange("e (p c) n -> e p (c n)", c=KC)
        wu_v = w_up.rearrange("e (p c) n -> e p (c n)", c=KC)
        wd_v = w_down.rearrange("e (h p c) n -> e h p (c n)", h=2, c=4)
        w_in_v = w_in.rearrange("(p c) n -> p c n", c=KC)

        def rounds_after_first(engine, body):
            engine.wait_ge(nr_ready, 1)
            rounds = engine.value_load(nr_i[0:1, 0:1], min_val=1, max_val=ROUNDS)
            with engine.If(rounds > 1):
                with engine.Fori(1, rounds) as r:
                    with engine.Fori(0, ITERS) as i:
                        body(i, r * ITERS + i)
            return rounds

        block = ctx.enter_context(nc.Block())

        @block.sync
        def _(sp_):
            for a in range(NT):
                sp_.dma_start(x3[:, a, :], x_d[a * P:(a + 1) * P, :]).then_inc(ld_x[a], 16)

            def small_loads():
                sp_.dma_start(cst2, const_d[:, C_TRI:C_KEEP]).then_inc(ld_const, 16)
                sp_.dma_start(rope_t, const_d[:, C_ROPE:C_ROPE + 192]).then_inc(ld_const, 16)
                sp_.dma_start(iota, const_d[:, C_IOTA:C_IOTA + SLOTS]).then_inc(ld_const, 16)
                sp_.dma_start(r_w[:, 0:C_END - C_KEEP], const_d[:, C_KEEP:C_END]).then_inc(ld_const2, 16)
                for w, b in enumerate((b_gate, b_up, b_down)):
                    sp_.dma_start(braw[:, w, :], b.rearrange("e (q n) -> (e q) n", n=BQ)).then_inc(ld_bias, 16)
                for k, v in enumerate((lam_q1, lam_k1, lam_q2, lam_k2)):
                    sp_.dma_start(lam_in[:, k * HD:(k + 1) * HD], v[0].partition_broadcast(P)).then_inc(ld_lam, 16)
                sp_.dma_start(g_rows, norm_ffn_g[0].rearrange("(c p) -> c p", c=KC)).then_inc(ld_gffn, 16)
                sp_.dma_start(g_sub[:, :], subln_g[0].rearrange("(p c) -> p c", c=1)).then_inc(ld_gsub, 16)

            def later_loads():
                sp_.dma_start(br[:, :], b_router[0].partition_broadcast(P)).then_inc(ld_router, 16)
                sp_.dma_start(wr3, w_router.rearrange("(c p) e -> p c e", c=KC)).then_inc(ld_router, 16)
                sp_.dma_start(gB, norm_ffn_g[0].partition_broadcast(P)).then_inc(ld_gB, 16)
                sp_.wait_ge(bias_parts, 5)
                for k in range(3):
                    for q in range(P // E):
                        sp_.dma_start(bias3[k * E:(k + 1) * E, :, q * BQ:(q + 1) * BQ],
                                      bpart[k][q:P:P // E, :, :]).then_inc(ld_bias3, 16)

            for n in range(HEAD_LOADS):
                if n == 2:
                    small_loads()
                if n == RING:
                    later_loads()
                s = n % RING
                if n >= RING:
                    sp_.wait_ge(step_done, STEP_OF_SLOT[n - RING] + 1)
                if n < 10:
                    col = STEP_COLS[STEP_OF_SLOT[n]]
                    sp_.dma_start(slot(s, KC, W512), w_in_v[:, :, col:col + W512]).then_inc(slot_loaded[s], 16)
                elif n >= 12:
                    cols = slice((n - 12) * W512, (n - 11) * W512)
                    sp_.dma_start(slot(s, KC, W512),
                                  w_o[:, cols].rearrange("(c p) n -> p c n", c=KC)).then_inc(slot_loaded[s], 16)
                else:
                    src = (w_sb_out, w_da_out)[n - 10]
                    sp_.dma_start(slot(s, 4, D), src.rearrange("(c p) n -> p c n", c=4)).then_inc(slot_loaded[s], 16)

            def load(i, p):
                e = i * (2 * PAIRS_PER_ITER) + 2 * (p // LOADS_PER_PAIR)
                m, s = p % LOADS_PER_PAIR, SLOT_OF[p]
                if m < 8:
                    src = (wg_v, wu_v)[m // 4][bass.ds(e, 2), :, (m % 4) * ROWS2:(m % 4 + 1) * ROWS2]
                else:
                    src = wd_v[bass.ds(e, 2), (m - 8) // 2, :, (m % 2) * ROWS2:(m % 2 + 1) * ROWS2]
                if m == LOADS_PER_PAIR - 1:
                    src = src.rearrange("k p (c n) -> k p c n", c=2)
                    for half, loaded in enumerate((slot_loaded[s], half_loaded[s])):
                        for k in range(2):
                            cols = slice(half * W512, (half + 1) * W512)
                            dst = expert_part(s, k).rearrange("p (c n) -> p c n", c=2)
                            sp_.dma_start(dst[:, :, cols], src[k, :, :, cols]).then_inc(loaded, 16)
                elif s <= RING:
                    dst = slot(s, 2, ROWS2) if s < RING else r_qk[:, :].rearrange("p (k n) -> p k n", k=2)
                    sp_.dma_start(dst, src.rearrange("k p n -> p k n")).then_inc(slot_loaded[s], 16)
                else:
                    for k in range(2):
                        sp_.dma_start(expert_part(s, k), src[k]).then_inc(slot_loaded[s], 16)

            def load_iteration(i, it):
                for p in range(LOADS_PER_ITER):
                    sp_.wait_ge(load_used, it * LOADS_PER_ITER + USED_BEFORE[p] + 1)
                    load(i, p)

            slot_free = {0: (step_done, GA0 + 1), 1: (step_done, GA1 + 1), 2: (step_done, GB0 + 1),
                         3: (step_done, GB1 + 1), 4: (yb_done, 4), 5: (ya_done, 4),
                         SLOT_OF.index(RING): (mix_ready, 4),
                         6: (wo_done, 2), 7: (wo_done, 3), SLOT_OF.index(RING + 1): (wo_done, 3),
                         SLOT_OF.index(RING + 2): (nr_ready, 1)}
            for p in FIRST_LOADS:
                sp_.wait_ge(*slot_free[p])
                if SLOT_OF[p] == RING + 1:
                    sp_.wait_ge(h_ready, 2)
                load(0, p)
            for p in range(LOADS_PER_ITER):
                if p not in FIRST_LOADS:
                    sp_.wait_ge(load_used, USED_BEFORE[p] + 1)
                    load(0, p)
            with sp_.Fori(1, ITERS) as i:
                load_iteration(i, i)
            rounds = rounds_after_first(sp_, load_iteration)
            sp_.wait_ge(gat_done, rounds * (2 * PAIRS) + 2)
            sp_.dma_start(gfin, norm_final_g.partition_broadcast(P)).then_inc(ld_gfin, 16)
            for a in range(NT):
                sp_.wait_ge(fin_done, a + 1)
                sp_.dma_start(out_d[a * P:(a + 1) * P, :], x3[:, a, :]).then_inc(stored, 16)
            sp_.wait_ge(stored, 16 * NT)

        @block.gpsimd
        def _(pool):
            nc.gpsimd.memset(eps, NORM_EPS)
            nc.gpsimd.memset(ones_row, 1.0).then_inc(zeroed, 1)
            nc.gpsimd.memset(qbz, 0.0).then_inc(zeroed, 1)
            nc.gpsimd.memset(qaz, 0.0).then_inc(zeroed, 1)
            pool.wait_ge(ld_const2, 16)
            stage = r_w[:, 0:C_END - C_KEEP]
            nc.gpsimd.tensor_copy(su_b[:, :], stage[:, C_SU - C_KEEP:C_SU - C_KEEP + P])
            nc.gpsimd.tensor_copy(one_b[:, :], stage[:, C_ONEP - C_KEEP:C_ONEP - C_KEEP + P])
            nc.gpsimd.tensor_copy(e3_b[:, :], stage[:, C_E3 - C_KEEP:C_END - C_KEEP]).then_inc(const_cast, 1)

            own = Steps(pool, bias_parts)
            pool.wait_ge(ld_bias, 16 * 3)
            own.step(nc.gpsimd.tensor_copy(bpart[0], braw))
            for k in (1, 2):
                own.settle()
                own.step(nc.gpsimd.tensor_tensor(braw, braw, bpart[k - 1], ALU.subtract))
                own.settle()
                own.step(nc.gpsimd.tensor_copy(bpart[k], braw))
            assert own.n == 5

        @block.scalar
        def _(act):
            own = Steps(act, act_own)
            act.dma_start(ident, const_d[:, C_ID:C_ID + P]).then_inc(ld_id, 16)
            act.dma_start(g_mix[:, :], norm_mix_g[0].rearrange("(p c) -> p c", c=KC)).then_inc(ld_gmix, 16)
            def root(a, b):
                return nc.scalar.activation(std[:, a:b], ssq[:, a:b], ACT.Sqrt, scale=1.0 / D, bias=eps)

            act.wait_ge(zeroed, 1)
            nc.scalar.activation(table_junk, ones_row[:, 0:2], ACT.Sqrt)

            act.wait_ge(ld_x[1], 16)
            nc.scalar.activation(r_a1[:, D:2 * D], x3[:, 1, :], ACT.Square, accum_out=ssq[:, 1:2]).then_inc(ssq1_ready, 1)
            act.wait_ge(ssq1_ready, 1)
            act.wait_ge(ssq0_ready, 1)
            root(0, NT).then_inc(std_ready, 1)
            act.wait_ge(rstd_ready, 1)
            nc.scalar.activation(xn3[:, 1, :], x3[:, 1, :], ACT.Copy, scale=rstd[:, 1:2]).then_inc(xn1_ready, 1)
            act.wait_ge(ld_gmix, 16)
            for b in (1, 3):
                act.wait_ge(hT_tr, b + 1)
                for c in (2 * b, 2 * b + 1):
                    nc.scalar.activation(hT[:, c, :], bank(b)[:, (c % 2) * T:(c % 2 + 1) * T], ACT.Copy,
                                         scale=g_mix[:, c:c + 1]).then_inc(hT_act, 1)
            act.wait_ge(lam_dot, 2)
            nc.scalar.activation(lam4[:, 2:4], lam4[:, 0:2], ACT.Exp).then_inc(lam_exp, 1)

            def wait_step(i):
                act.wait_ge(step_done, i + 1)

            def pair_banks(i, lo=0, hi=P):
                return ps[lo:hi, (i % 2) * 2 * W512:((i % 2) * 2 + 2) * W512]

            wait_step(QB)
            act.wait_ge(zeroed, 2)
            nc.scalar.activation(qbz[HD:P, 1::2, :], pair_banks(QB, HD, P).rearrange("p (c t) -> p c t", c=4), ACT.Copy,
                                 scale=Q_SCALE).then_inc(evac[QB], 1)
            wait_step(KB)
            nc.scalar.copy(r_kv[:, 0:1024], pair_banks(KB)).then_inc(evac[KB], 1)
            wait_step(VB)
            nc.scalar.copy(r_kv[:, 1024:2048], pair_banks(VB)).then_inc(evac[VB], 1)

            def softplus_part(g):
                act.wait_ge(sb_abs, 4 * (g + 1))
                own.step(nc.scalar.activation(sp[:, :, :], sp[:, :, :], ACT.Exp))
                own.settle()
                nc.scalar.activation(sp[:, :, :], sp[:, :, :], ACT.Ln, bias=1.0).then_inc(sb_ln, 1)

            def stick_exp(g):
                act.wait_ge(sb_arg, 4 * (g + 1))
                nc.scalar.activation(zb[:, :, :], zb[:, :, :], ACT.Exp).then_inc(sb_a, 1)

            def stick_out(g):
                act.wait_ge(sb_o, g + 1)
                act.wait_ge(bias_parts, 5)
                nc.scalar.copy(obT[:, 2 * g:2 * g + 2, :], bank(4).rearrange("p (c t) -> p c t", c=2)).then_inc(sb_ev, 1)

            softplus_part(0)
            wait_step(TRQ)
            act.wait_ge(zeroed, 3)
            nc.scalar.activation(qaz[HD:P, 1::2, :], pair_banks(TRQ, HD, P).rearrange("p (c t) -> p c t", c=4),
                                 ACT.Copy, scale=Q_SCALE).then_inc(evac[TRQ], 1)
            stick_exp(0)
            wait_step(VA)
            nc.scalar.copy(r_va[:, :], pair_banks(VA)).then_inc(evac[VA], 1)
            stick_out(0)
            wait_step(TRK)
            nc.scalar.copy(r_ka[:, 0:W512], pair_banks(TRK)[:, 0:W512]).then_inc(evac[TRK], 1)
            softplus_part(1)

            def sigmoid_of(i, dst, half):
                wait_step(i)
                nc.scalar.activation(dst[:, 4 * half:4 * half + 4, :], pair_banks(i).rearrange("p (c t) -> p c t", c=4),
                                     ACT.Sigmoid).then_inc(evac[i], 1)

            sigmoid_of(GA0, sga, 0)
            stick_exp(1)
            sigmoid_of(GA1, sga, 1)
            stick_out(1)
            for h in range(HEADS):
                act.wait_ge(da_nm, h + 1)
                nc.scalar.activation(pb[:, h, 0:P], pb[:, h, 0:P], ACT.Exp, bias=nmx[:, h, 0:1],
                                     accum_out=den[:, h, 0:1])
                nc.scalar.activation(pb[:, h, P:BLOCKS], pb[:, h, P:BLOCKS], ACT.Exp, bias=nmx[:, h, 1:2],
                                     accum_out=den[:, h, 1:2]).then_inc(da_e, 1)
            sigmoid_of(GB0, sgb, 0)
            sigmoid_of(GB1, sgb, 1)

            def head_squares(heads):
                act.wait_ge(da_o, heads[-1] + 1)
                for hd, a in ((hd, a) for hd in heads for a in range(NT)):
                    c0 = (hd % 2) * T + a * P
                    junk = 2 * (hd % 2) + a
                    last = nc.scalar.activation(r_tb[:, junk * P:(junk + 1) * P], bank(6 + hd // 2)[:, c0:c0 + P],
                                                ACT.Square,
                                                accum_out=ossq[:, 2 * hd + a:2 * hd + a + 1])
                last.then_inc(da_ssq, 1)

            act.wait_ge(ld_bias3, 16 * 12)
            for hd in range(DA_HEADS):
                act.wait_ge(da_t, hd + 1)
                if hd >= 2:
                    act.wait_ge(da_o, hd - 1)
                nc.scalar.copy(wT[:, hd % 2, :], bank(4 + hd % 2)[:, 0:BLOCKS]).then_inc(da_wt, 1)
            head_squares((0, 1))
            act.wait_ge(da_ssq, 1)
            head_squares((2, 3))
            act.wait_ge(da_var, 1)
            nc.scalar.activation(ossq, ossq, ACT.Sqrt).then_inc(da_std, 1)
            act.wait_ge(tro, 1)
            nc.scalar.activation(oT[:, 0:2, :], bank(4).rearrange("p (c t) -> p c t", c=2), ACT.Copy,
                                 scale=g_sub8).then_inc(oT_act, 1)

            def router_input(a, b):
                act.wait_ge(tx_done, 2 * a + b + 1)
                act.wait_ge(ld_router, 16 * 2)
                for c in range(4):
                    last = nc.scalar.activation(hTr[a][:, 4 * b + c, :], bank(4 + 2 * a + b)[:, c * P:(c + 1) * P],
                                                ACT.Copy, scale=g_ffn[:, 4 * b + c:4 * b + c + 1])
                last.then_inc(hTr_act, 1)

            def h_part(a, w, b, ready, done):
                act.wait_ge(ready, 2 * a + b + 1)
                nc.scalar.copy(h3[:, a, w, 4 * b:4 * b + 4], h32[a][:, 4 * b:4 * b + 4]).then_inc(done, 1)

            def logits_out(a):
                act.wait_ge(rt_done, a + 1)
                nc.scalar.copy(lT[0:E, a * P:(a + 1) * P], bank(4 * a)[0:E, 0:P]).then_inc(lT_ready, 1)

            act.wait_ge(x1, 1)
            nc.scalar.activation(r_va[:, :], x3[:, 0, :], ACT.Square, accum_out=ssq[:, 0:1]).then_inc(ssq2_ready, 1)
            act.wait_ge(ssq2_ready, 1)
            root(0, 1).then_inc(std2_ready, 1)
            router_input(0, 1)
            h_part(0, 0, 0, h_full, h_p1)
            h_part(0, 0, 1, h_full, h_p1)
            logits_out(0)
            h_part(0, 1, 0, h_r1, h_p2)
            h_part(0, 1, 1, h_r1, h_p2)
            act.wait_ge(x1, 2)
            nc.scalar.activation(r_va[:, 0:W512], x3[:, 1, 0:W512], ACT.Square, accum_out=ssq_half).then_inc(ssq2_ready, 1)
            router_input(1, 0)
            act.wait_ge(x1, 3)
            act.wait_ge(ssq2_ready, 2)
            nc.scalar.activation(r_va[:, 0:W512], x3[:, 1, W512:D], ACT.Square,
                                 accum_out=ssq[:, 1:2]).then_inc(ssq2_ready, 1)
            act.wait_ge(ssq2_ready, 3)
            act.wait_ge(bias_ready, 1)
            nc.scalar.activation(std[:, 1:2], ssq[:, 1:2], ACT.Sqrt, scale=1.0 / D, bias=root_bias).then_inc(std2_ready, 1)
            h_part(1, 0, 0, h_full, h_p1)
            logits_out(1)
            h_part(1, 0, 1, h_full, h_p1)
            h_part(1, 1, 0, h_r1, h_p2)
            h_part(1, 1, 1, h_r1, h_p2)
            for a in range(NT):
                act.wait_ge(neg_top, a + 1)
                nc.scalar.activation(ex[:, a, :], lg[:, a, :], ACT.Exp, bias=rt[:, 4 + a:5 + a]).then_inc(ex_ready, 1)

            def gathered(n_value):
                for b in range(2):
                    act.wait_ge(gat_done, n_value * 2 - 1 + b)
                    nc.scalar.copy(xT[:, 4 * b:4 * b + 4, :],
                                   bank(T_B + b).rearrange("p (c s) -> p c s", c=4)).then_inc(xT_ready, 1)

            gathered(1)

            def expert_iteration(i, it):
                for q in range(PAIRS_PER_ITER):
                    n = it * PAIRS_PER_ITER + q
                    act.wait_ge(g_clipped, n + 1)
                    nc.scalar.activation(sg_s, g_s, ACT.Sigmoid, scale=ALPHA).then_inc(sig_ready, 1)
                    gathered(n + 2)
                    act.wait_ge(gt_done, n + 1)
                    nc.scalar.copy(g_T, bank(O_B)[:, 0:T]).then_inc(gt_ready, 1)
                    for b in range(2):
                        act.wait_ge(ht_done, n * 2 + b + 1)
                        nc.scalar.copy(hTm[:, 4 * b:4 * b + 4, :],
                                       bank(T_B + b).rearrange("p (c s) -> p c s", c=4)).then_inc(hT_ready, 1)
                    for b in range(2):
                        if b == 0:
                            act.wait_ge(down_done, n + 1)
                        else:
                            act.wait_ge(load_used, it * LOADS_PER_ITER + LOADS_PER_PAIR * (q + 1))
                        nc.scalar.copy(o_s[:, b * W512:(b + 1) * W512], bank(O_B + b)).then_inc(o_ready, 1)

            with act.Fori(0, ITERS) as i:
                expert_iteration(i, i)
            rounds = rounds_after_first(act, expert_iteration)
            nc.scalar.activation(table_junk, ones_row[:, 0:2], ACT.Sqrt)
            act.wait_ge(y_added, rounds * (4 * PAIRS) + 1)
            nc.scalar.activation(r_va[:, :], x3[:, 1, :], ACT.Square, accum_out=ssq[:, 1:2]).then_inc(ssq1_ready, 1)
            act.wait_ge(ssq1_ready, 2)
            act.wait_ge(ssq0_ready, 2)
            root(0, NT).then_inc(fin_std, 1)

        @block.vector
        def _(dve):
            own = Steps(dve, dve_own)

            def square_sum(junk, a):
                return nc.vector.tensor_tensor_reduce(out=junk, in0=x3[:, a, :], in1=x3[:, a, :], scale=1.0, scalar=0.0,
                                                      op0=ALU.mult, op1=ALU.add, accum_out=ssq[:, a:a + 1])

            dve.wait_ge(ld_x[0], 16)
            square_sum(r_a1[:, 0:D], 0).then_inc(ssq0_ready, 1)
            dve.wait_ge(std_ready, 1)
            nc.vector.reciprocal(rstd, std).then_inc(rstd_ready, 1)
            dve.wait_ge(rstd_ready, 1)
            nc.vector.tensor_scalar(xn3[:, 0, :], x3[:, 0, :], rstd[:, 0:1], None, ALU.mult).then_inc(xn_ready, 1)
            dve.wait_ge(ld_gmix, 16)
            for b in (0, 2):
                dve.wait_ge(hT_tr, b + 1)
                for c in (2 * b, 2 * b + 1):
                    nc.vector.tensor_scalar(hT[:, c, :], bank(b)[:, (c % 2) * T:(c % 2 + 1) * T], g_mix[:, c:c + 1],
                                            None, ALU.mult).then_inc(hT_dve, 1)
            dve.wait_ge(ld_lam, 16 * 4)
            dve.wait_ge(ld_gsub, 16)
            for k in range(2):
                nc.vector.tensor_tensor_reduce(
                    out=r_w[:, 2048 + k * HD:2048 + (k + 1) * HD], in0=lam_in[:, 2 * k * HD:(2 * k + 1) * HD],
                    in1=lam_in[:, (2 * k + 1) * HD:(2 * k + 2) * HD], scale=1.0, scalar=0.0, op0=ALU.mult, op1=ALU.add,
                    accum_out=lam4[:, k:k + 1]).then_inc(lam_dot, 1)
            dve.wait_ge(lam_exp, 1)
            own.step(nc.vector.tensor_tensor(lamv[:, 0:1], lam4[:, 2:3], lam4[:, 3:4], ALU.subtract))
            own.step(nc.vector.tensor_scalar(g_sub8, g_sub[:, :], 1.0 - LAMBDA_INIT, None, ALU.mult))
            own.settle()
            own.step(nc.vector.tensor_scalar(lamv[:, 1:2], lamv[:, 0:1], LAMBDA_INIT, -1.0, ALU.add, ALU.mult))
            own.settle()

            def wait_step(i):
                dve.wait_ge(step_done, i + 1)

            def pair_banks(i, lo=0, hi=P):
                return ps[lo:hi, (i % 2) * 2 * W512:((i % 2) * 2 + 2) * W512]

            wait_step(QB)
            dve.wait_ge(zeroed, 2)
            nc.vector.tensor_scalar(qbz[0:HD, 0::2, :], pair_banks(QB, 0, HD).rearrange("p (c t) -> p c t", c=4),
                                    Q_SCALE, None, ALU.mult).then_inc(evac[QB], 1)
            dve.wait_ge(g_tr, 1)
            nc.vector.tensor_copy(g_ffn[:, :], bank(4)[:, 0:KC]).then_inc(g_cols, 1)
            dve.wait_ge(ld_const, 16 * 3)
            dve.wait_ge(const_cast, 1)

            def stick_scores(g):
                if g:
                    dve.wait_ge(sb_o, g)
                for hh in range(4):
                    dve.wait_ge(sb_z, 4 * g + hh + 1)
                    z = bank(4 + hh)[:, 0:BLOCKS].rearrange("p (b n) -> p b n", b=3)
                    o = zb[:, hh, :].rearrange("p (b n) -> p b n", b=3)
                    own.step(nc.vector.tensor_tensor(o[:, 0::2, :], z[:, 0::2, :],
                                                     mask_sb.unsqueeze(1).to_broadcast([P, 2, P]), ALU.add))
                    own.step(nc.vector.tensor_copy(o[:, 1, :], z[:, 1, :]))
                    own.settle()
                    nc.vector.scalar_tensor_tensor(out=sp[:, hh, :], in0=zb[:, hh, :], scalar=-1.0, in1=zb[:, hh, :],
                                                   op0=ALU.mult, op1=ALU.min).then_inc(sb_abs, 1)

            def stick_softplus(g):
                dve.wait_ge(sb_ln, g + 1)
                nc.vector.scalar_tensor_tensor(out=r_w[:, 4 * BLOCKS:8 * BLOCKS], in0=r_w[:, 0:4 * BLOCKS], scalar=0.0,
                                               in1=r_w[:, 4 * BLOCKS:8 * BLOCKS], op0=ALU.max,
                                               op1=ALU.add).then_inc(sb_sp, 1)

            def stick_argument(g):
                for hh in range(4):
                    dve.wait_ge(sb_r, 4 * g + hh + 1)
                    nc.vector.tensor_tensor(zb[:, hh, :], bank(4 + hh)[:, 0:BLOCKS], zb[:, hh, :],
                                            ALU.add).then_inc(sb_arg, 1)

            def rotate(i):
                wait_step(i)
                if i == KA:
                    dve.wait_ge(step_done, TRQ + 1)
                xs = pair_banks(i).rearrange("p (a h w d) -> p a h w d", a=NT, h=HEADS, w=2)
                tb = r_tb[:, :].rearrange("p (h w d) -> p h w d", h=HEADS, w=2)
                for a in range(NT):
                    cos, sin, nsin = (rope[:, a, w, :] for w in range(3))
                    ra = rot[:, a, :]
                    own.settle()
                    nc.vector.tensor_tensor(ra.rearrange("p (m d) -> p m d", d=HD // 2),
                                            xs[:, a].rearrange("p h w d -> p (h w) d"),
                                            cos.unsqueeze(1).to_broadcast([P, 2 * HEADS, HD // 2]), ALU.mult)
                    nc.vector.tensor_tensor(tb[:, :, 0, :], xs[:, a, :, 1, :],
                                            nsin.unsqueeze(1).to_broadcast([P, HEADS, HD // 2]), ALU.mult)
                    last = nc.vector.tensor_tensor(tb[:, :, 1, :], xs[:, a, :, 0, :],
                                                   sin.unsqueeze(1).to_broadcast([P, HEADS, HD // 2]), ALU.mult)
                    own.step(last)
                    own.settle()
                    add = nc.vector.tensor_tensor(ra, ra, r_tb[:, :], ALU.add)
                    if a == NT - 1:
                        add.then_inc(rope_done, 1)
                        nc.vector.engine_nop().then_inc(evac[i], 1)
                    else:
                        own.step(add)

            stick_scores(0)
            stick_softplus(0)
            dve.wait_ge(zeroed, 3)
            dve.wait_ge(ld_bias3, 16 * 12)
            rotate(QA)
            rotate(KA)
            nc.vector.tensor_scalar(qaz[0:HD, 0::2, :], pair_banks(TRQ, 0, HD).rearrange("p (c t) -> p c t", c=4),
                                    Q_SCALE, None, ALU.mult).then_inc(evac[TRQ], 1)
            stick_argument(0)
            wait_step(TRK)
            nc.vector.tensor_copy(r_ka[:, W512:2 * W512], pair_banks(TRK)[:, W512:2 * W512]).then_inc(evac[TRK], 1)
            stick_scores(1)
            stick_softplus(1)
            stick_argument(1)

            dve.wait_ge(sb_o, 2)
            for h in range(HEADS):
                dve.wait_ge(da_s, h + 1)
                s = bank(4 + h % 4)
                own.step(nc.vector.tensor_tensor_reduce(
                    out=pb[:, h, 0:P], in0=s[:, 0:P], in1=mask_da[:, P:2 * P], scale=1.0, scalar=-3e38, op0=ALU.add,
                    op1=ALU.max, accum_out=mx[:, h, 0:1]))
                nc.vector.tensor_tensor_reduce(
                    out=pb[:, h, P:BLOCKS], in0=s[:, P:BLOCKS], in1=mask_da, scale=1.0, scalar=-3e38, op0=ALU.add,
                    op1=ALU.max, accum_out=mx[:, h, 1:2]).then_inc(da_read, 1)
                own.settle()
                dve.wait_ge(da_read, h + 1)
                nc.vector.tensor_scalar(nmx[:, h, :], mx[:, h, :], -1.0, None, ALU.mult).then_inc(da_nm, 1)
            for hd in range(DA_HEADS):
                h1, h2 = 2 * hd, 2 * hd + 1
                dve.wait_ge(da_e, h2 + 1)
                own.step(nc.vector.reciprocal(rden[:, h1:h2 + 1, :], den[:, h1:h2 + 1, :]))
                own.settle()
                own.step(nc.vector.tensor_scalar(c2[:, hd, :], rden[:, h2, :], lamv[:, 1:2], None, ALU.mult))
                own.settle()
                spans = ((0, P), (P, BLOCKS))
                for a, (lo, hi) in enumerate(spans):
                    own.step(nc.vector.tensor_scalar(pb[:, h2, lo:hi], pb[:, h2, lo:hi], c2[:, hd, a:a + 1], None,
                                                     ALU.mult))
                own.settle()
                for a, (lo, hi) in enumerate(spans):
                    last = nc.vector.scalar_tensor_tensor(out=pb[:, h1, lo:hi], in0=pb[:, h1, lo:hi],
                                                          scalar=rden[:, h1, a:a + 1], in1=pb[:, h2, lo:hi],
                                                          op0=ALU.mult, op1=ALU.add)
                last.then_inc(da_w, 1)
            dve.wait_ge(da_ssq, 2)
            nc.vector.tensor_scalar(ossq, ossq, 1.0 / P, NORM_EPS, ALU.mult, ALU.add).then_inc(da_var, 1)
            dve.wait_ge(da_std, 1)
            own.step(nc.vector.reciprocal(orstd, ossq))
            own.settle()
            for hd in range(DA_HEADS):
                for a in range(NT):
                    c0 = (hd % 2) * T + a * P
                    last = nc.vector.tensor_scalar(on3[:, a, hd * P:(hd + 1) * P], bank(6 + hd // 2)[:, c0:c0 + P],
                                                   orstd[:, 2 * hd + a:2 * hd + a + 1], None, ALU.mult)
            last.then_inc(on_ready, 1)
            dve.wait_ge(tro, 1)
            nc.vector.tensor_scalar(oT[:, 2:4, :], bank(5).rearrange("p (c t) -> p c t", c=2), g_sub8, None,
                                    ALU.mult).then_inc(oT_dve, 1)
            dve.wait_ge(evac[GB1], 1)
            for b in range(4):
                dve.wait_ge(yb_done, b + 1)
                own.step(nc.vector.tensor_tensor(r_qa[:, b * W512:(b + 1) * W512], bank(b),
                                                 r_qa[:, b * W512:(b + 1) * W512], ALU.mult))
            for b in range(4):
                dve.wait_ge(ya_done, b + 1)
                cols = slice(b * W512, (b + 1) * W512)
                own.step(nc.vector.tensor_tensor(r_a1[:, cols], bank(4 + b), r_a2[:, cols], ALU.mult))
                own.settle()
                nc.vector.tensor_tensor(r_a1[:, cols], r_a1[:, cols], r_qa[:, cols], ALU.add).then_inc(mix_ready, 1)
            def residual(a, halves):
                for half in halves:
                    cols = slice(half * W512, (half + 1) * W512)
                    last = nc.vector.tensor_tensor(x3[:, a, cols], bank(2 * a + half), x3[:, a, cols], ALU.add)
                last.then_inc(x1, 1)

            def router_input(a, b):
                dve.wait_ge(tx_done, 2 * a + b + 1)
                dve.wait_ge(ld_router, 16 * 2)
                nc.vector.tensor_tensor(hTr[a][:, 4 * b:4 * b + 4, :],
                                        bank(4 + 2 * a + b).rearrange("p (c t) -> p c t", c=4),
                                        g_ffn[:, 4 * b:4 * b + 4].unsqueeze(2).to_broadcast([P, 4, P]),
                                        ALU.mult).then_inc(hTr_dve, 1)

            def h_float(a):
                dve.wait_ge(std2_ready, a + 1)
                own.step(nc.vector.reciprocal(rstd[:, a:a + 1], std[:, a:a + 1]))
                own.settle()
                dve.wait_ge(ld_gB, 16)
                for b in range(2):
                    cs = slice(4 * b, 4 * b + 4)
                    nc.vector.scalar_tensor_tensor(
                        out=h32[a][:, cs], in0=x3[:, a, :].rearrange("p (m c) -> p c m", c=KC)[:, cs],
                        scalar=rstd[:, a:a + 1], in1=gB.rearrange("p (m c) -> p c m", c=KC)[:, cs], op0=ALU.mult,
                        op1=ALU.mult).then_inc(h_full, 1)

            def h_rest(a):
                for b in range(2):
                    cs = slice(4 * b, 4 * b + 4)
                    dve.wait_ge(h_p1, 2 * a + b + 1)
                    nc.vector.tensor_tensor(h32[a][:, cs], h32[a][:, cs], h3[:, a, 0, cs], ALU.subtract).then_inc(h_r1, 1)

            def h_last_part(a):
                for b in range(2):
                    cs = slice(4 * b, 4 * b + 4)
                    dve.wait_ge(h_p2, 2 * a + b + 1)
                    dve.wait_ge(h_r1, 2 * a + b + 1)
                    nc.vector.tensor_tensor(h3[:, a, 2, cs], h32[a][:, cs], h3[:, a, 1, cs], ALU.subtract).then_inc(h_ready, 1)

            def choose(a):
                dve.wait_ge(rt_tr, a + 1)
                own.step(nc.vector.scalar_tensor_tensor(out=lg[:, a, :], in0=bank(1 + 4 * a)[:, 0:E],
                                                        scalar=rstd[:, a:a + 1], in1=br[:, :], op0=ALU.mult,
                                                        op1=ALU.add))
                own.settle()
                own.step(nc.vector.max(top8[:, a, :], lg[:, a, :]))
                own.settle()
                fourth = top8[:, a, TOP_K - 1:TOP_K]
                own.step(nc.vector.tensor_scalar(eq[:, a, :], lg[:, a, :], fourth, None, ALU.is_equal))
                own.step(nc.vector.tensor_scalar(gt[:, a, :], lg[:, a, :], fourth, 0.0, ALU.is_gt, ALU.add,
                                                 accum_out=rt[:, a:a + 1]))
                nc.vector.tensor_scalar(rt[:, 4 + a:5 + a], top8[:, a, 0:1], -1.0, None, ALU.mult).then_inc(neg_top, 1)
                own.settle()
                own.step(nc.vector.tensor_tensor_scan(cum[:, a, :], ones_row, eq[:, a, :], 0.0, ALU.mult, ALU.add))
                own.step(nc.vector.tensor_scalar(rt[:, 2 + a:3 + a], rt[:, a:a + 1], -1.0, TOP_K + 0.5, ALU.mult,
                                                 ALU.add))
                own.settle()
                own.step(nc.vector.scalar_tensor_tensor(out=eq[:, a, :], in0=cum[:, a, :], scalar=rt[:, 2 + a:3 + a],
                                                        in1=eq[:, a, :], op0=ALU.is_lt, op1=ALU.mult))
                own.settle()
                nc.vector.tensor_tensor(mask_b[:, a, :], eq[:, a, :], gt[:, a, :], ALU.add).then_inc(mask_ready, 1)
                own.step(nc.vector.tensor_tensor(mask[:, a, :], eq[:, a, :], gt[:, a, :], ALU.add))

            dve.wait_ge(wo_done, 1)
            residual(0, (0, 1))
            router_input(0, 0)
            h_float(0)
            h_rest(0)
            dve.wait_ge(wo_done, 2)
            residual(1, (0,))
            choose(0)
            h_last_part(0)
            dve.wait_ge(ssq2_ready, 2)
            nc.vector.tensor_scalar(root_bias, ssq_half, 1.0 / D, NORM_EPS, ALU.mult, ALU.add).then_inc(bias_ready, 1)
            dve.wait_ge(wo_done, 3)
            residual(1, (1,))
            router_input(1, 1)
            h_float(1)
            h_rest(1)
            choose(1)
            h_last_part(1)
            own.settle()
            dve.wait_ge(rk_done, 1)
            own.step(nc.vector.scalar_tensor_tensor(
                out=rkx[:, :, 0:E], in0=bank(2)[:, 0:2 * E].rearrange("p (a e) -> p a e", a=NT), scalar=1.0,
                in1=mask, op0=ALU.add, op1=ALU.mult))
            own.settle()

            def select(q, n):
                for k in range(2):
                    for a in range(NT):
                        nc.vector.tensor_scalar(s_sel[:, a, k * SLOTS:(k + 1) * SLOTS], iota,
                                                rkx[:, a, bass.ds(n * 2 + k, 1)], None, ALU.is_equal)
                    last = nc.vector.tensor_copy(oh[q][0:3 * E, k * SLOTS:(k + 1) * SLOTS],
                                                 e3_b[0:3 * E, bass.ds(n * 2 + k, 1)].to_broadcast([3 * E, SLOTS]))
                last.then_inc(sel_ready, 1)

            select(0, 0)
            for a in range(NT):
                dve.wait_ge(ex_ready, a + 1)
                own.step(nc.vector.tensor_tensor_reduce(out=ex[:, a, :], in0=ex[:, a, :], in1=mask[:, a, :], scale=1.0,
                                                        scalar=0.0, op0=ALU.mult, op1=ALU.add,
                                                        accum_out=rt[:, 6 + a:7 + a]))
            own.settle()
            own.step(nc.vector.reciprocal(rt[:, 8:10], rt[:, 6:8]))
            own.settle()
            for a in range(NT):
                own.step(nc.vector.tensor_scalar(gates[:, a, :], ex[:, a, :], rt[:, 8 + a:9 + a], None, ALU.mult))
            own.step(nc.vector.reduce_max(rt[:, 10:11], bank(2)[:, 2 * E:3 * E], AX.X))
            own.step(nc.vector.memset(rkx[:, :, ROUNDS * E:N_ROUND_COLS], -1.0))
            own.step(nc.vector.memset(gx[:, :, ROUNDS * E:N_ROUND_COLS], 0.0))
            own.settle()
            for r in range(ROUNDS):
                if r:
                    own.step(nc.vector.tensor_scalar(rkx[:, :, r * E:(r + 1) * E], rkx[:, :, 0:E],
                                                     -float(SLOTS * r), None, ALU.add))
                own.step(nc.vector.tensor_copy(gx[:, :, r * E:(r + 1) * E], gates))
            for r in range(ROUNDS):
                own.step(nc.vector.tensor_scalar(nrd[:, r:r + 1], rt[:, 10:11], float(SLOTS * r) if r else -1.0, None,
                                                 ALU.is_gt))
            own.settle()
            own.step(nc.vector.tensor_reduce(rt[:, 11:12], nrd, AX.X, ALU.add))
            own.settle()
            nc.vector.tensor_copy(nr_i[:, :], rt[:, 11:12]).then_inc(nr_ready, 1)
            dve.wait_ge(x1, 3)
            nc.vector.engine_nop().then_inc(y_added, 1)
            base = own.n

            def expert_iteration(i, it):
                steps = Steps(dve, dve_own, it * DVE_STEPS_PER_ITER + base)
                for q in range(PAIRS_PER_ITER):
                    n = it * PAIRS_PER_ITER + q
                    dve.wait_ge(load_used, it * LOADS_PER_ITER + LOADS_PER_PAIR * q + 4)
                    nc.vector.tensor_scalar(g_s, bank(G_B, 2), LIMIT, None, ALU.min).then_inc(g_clipped, 1)
                    for k in range(2):
                        for a in range(NT):
                            last = nc.vector.tensor_scalar(gs[:, a, k * SLOTS:(k + 1) * SLOTS], iota,
                                                           rkx[:, a, bass.ds(n * 2 + k, 1)],
                                                           gx[:, a, bass.ds(n * 2 + k, 1)], ALU.is_equal, ALU.mult)
                    last.then_inc(gs_ready, 1)
                    select((q + 1) % 2, n + 1)
                    dve.wait_ge(sig_ready, n + 1)
                    steps.step(nc.vector.tensor_tensor(g_s, g_s, sg_s, ALU.mult))
                    steps.settle()
                    dve.wait_ge(load_used, it * LOADS_PER_ITER + LOADS_PER_PAIR * q + 8)
                    steps.step(nc.vector.tensor_scalar(u_s, bank(U_B, 2), LIMIT, -LIMIT, ALU.min, ALU.max))
                    steps.settle()
                    nc.vector.scalar_tensor_tensor(out=g_s, in0=u_s, scalar=1.0, in1=g_s, op0=ALU.add,
                                                   op1=ALU.mult).then_inc(act_ready, 1)
                    dve.wait_ge(y_added, n * 4 + 1)
                    for half, b in ((0, U_B), (1, T_B)):
                        dve.wait_ge(sc_done, n * 2 + half + 1)
                        for a in range(NT):
                            cols = slice(half * W512, (half + 1) * W512)
                            nc.vector.tensor_tensor(x3[:, a, cols], bank(b + a), x3[:, a, cols],
                                                    ALU.add).then_inc(y_added, 1)
                assert steps.n == DVE_STEPS_PER_ITER

            with dve.Fori(0, ITERS) as i:
                expert_iteration(i, i)
            rounds = rounds_after_first(dve, expert_iteration)

            dve.wait_ge(y_added, rounds * (4 * PAIRS) + 1)
            square_sum(r_a1[:, 0:D], 0).then_inc(ssq0_ready, 1)
            dve.wait_ge(fin_std, 1)
            nc.vector.reciprocal(rstd, std).then_inc(rstd_ready, 1)
            dve.wait_ge(rstd_ready, 2)
            dve.wait_ge(ld_gfin, 16)
            for a in range(NT):
                nc.vector.scalar_tensor_tensor(out=x3[:, a, :], in0=x3[:, a, :], scalar=rstd[:, a:a + 1], in1=gfin,
                                               op0=ALU.mult, op1=ALU.mult).then_inc(fin_done, 1)

        @block.tensor
        def _(pe):
            mm = nc.tensor.matmul

            def wait_slot(n):
                pe.wait_ge(slot_loaded[n % RING], 16 * (n // RING + 1))

            pe.wait_ge(ld_id, 16)
            pe.wait_ge(xn_ready, 1)
            pe.wait_ge(xn1_ready, 1)
            for c in range(KC):
                for a in range(NT):
                    last = nc.tensor.transpose(bank(c // 2)[:, (c % 2) * T + a * P:(c % 2) * T + (a + 1) * P],
                                               xn3[:, a, c:D:KC], ident)
                if c % 2:
                    last.then_inc(hT_tr, 1)
            pe.wait_ge(hT_dve, KC // 2)
            pe.wait_ge(hT_act, KC // 2)

            def project(i):
                n = STEP_SLOT[i]
                wait_slot(n)
                if i >= 2:
                    pe.wait_ge(evac[i - 2], EVACUATIONS[i - 2])
                w = slot(n % RING, KC, W512)
                b = (i % 2) * 2
                if i in (VB, QA, KA, VA):
                    for a in range(NT):
                        for c in range(KC):
                            last = mm(bank(b + a), hT[:, c, a * P:(a + 1) * P], w[:, c, :], start=c == 0, stop=c == KC - 1)
                else:
                    for j in range(4):
                        for c in range(KC):
                            last = mm(bank(b + j // 2)[:, (j % 2) * T:(j % 2 + 1) * T], w[:, c, j * P:(j + 1) * P],
                                      hT[:, c, :], start=c == 0, stop=c == KC - 1)
                last.then_inc(step_done, 1)

            def transpose_heads(i, rotated):
                pe.wait_ge(rope_done, rotated)
                pe.wait_ge(evac[i - 2], EVACUATIONS[i - 2])
                for j in range(4):
                    for a in range(NT):
                        c0 = (i % 2) * 2 * W512 + j * T + a * P
                        last = nc.tensor.transpose(ps[:, c0:c0 + P], rot[:, a, j * P:(j + 1) * P], ident)
                last.then_inc(step_done, 1)

            def stick_scores(g):
                for hh in range(4):
                    h = 4 * g + hh
                    mm(bank(4 + hh)[:, 0:T], kbT[:, h // 2, 0:P], qbz[:, h, :], start=True, stop=True)
                    mm(bank(4 + hh)[:, T:BLOCKS], kbT[:, h // 2, P:T], qbz[:, h, P:T], start=True,
                       stop=True).then_inc(sb_z, 1)

            def stick_sums(g):
                pe.wait_ge(sb_sp, g + 1)
                for hh in range(4):
                    b = bank(4 + hh)
                    mm(b[:, 0:BLOCKS], tri_neg, sp[:, hh, :], start=True, stop=False)
                    mm(b[:, P:T], one_neg, sp[:, hh, T:BLOCKS], start=False, stop=True).then_inc(sb_r, 1)

            def stick_values(g):
                pe.wait_ge(sb_a, g + 1)
                for hh in (0, 2):
                    pair = [(j, 4 * g + j, bank(4)[j % 2 * HD:(j % 2 + 1) * HD, (j // 2) * T:(j // 2 + 1) * T])
                            for j in (hh, hh + 1)]
                    for j, h, o in pair:
                        mm(o, vb3[:, 0, h * HD:(h + 1) * HD], zb[:, j, 0:T], start=True, stop=False)
                    for j, h, o in pair:
                        last = mm(o[:, P:T], vb3[:, 1, h * HD:(h + 1) * HD], zb[:, j, T:BLOCKS], start=False,
                                  stop=True)
                last.then_inc(sb_o, 1)

            project(QB)
            project(KB)
            pe.wait_ge(ld_gffn, 16)
            nc.tensor.transpose(bank(4)[:, 0:KC], g_rows, ident[0:KC, 0:KC]).then_inc(g_tr, 1)
            project(VB)
            pe.wait_ge(g_cols, 1)
            pe.wait_ge(evac[KB], 1)
            stick_scores(0)
            project(QA)
            project(KA)
            transpose_heads(TRQ, 1)
            stick_sums(0)
            project(VA)
            stick_values(0)
            transpose_heads(TRK, 2)
            pe.wait_ge(sb_ev, 1)
            stick_scores(1)
            project(GA0)
            stick_sums(1)
            project(GA1)
            stick_values(1)
            pe.wait_ge(evac[TRQ], 2)
            pe.wait_ge(evac[TRK], 2)
            pe.wait_ge(sb_ev, 2)
            for h in range(HEADS):
                if h >= 4:
                    pe.wait_ge(da_read, h - 3)
                s = bank(4 + h % 4)
                mm(s[:, 0:P], qaz[:, h, 0:P], kaT[:, h // 2, 0:P], start=True, stop=True)
                mm(s[:, P:BLOCKS], qaz[:, h, P:T], kaT[:, h // 2, :], start=True, stop=True).then_inc(da_s, 1)
            project(GB0)
            project(GB1)

            def transpose_weights(hd):
                pe.wait_ge(da_w, hd + 1)
                if hd >= 2:
                    pe.wait_ge(da_wt, hd - 1)
                else:
                    pe.wait_ge(da_read, HEADS)
                for k in range(3):
                    last = nc.tensor.transpose(bank(4 + hd % 2)[:, k * P:(k + 1) * P], pb[:, 2 * hd, k * P:(k + 1) * P],
                                               ident)
                last.then_inc(da_t, 1)

            def head_values(hd):
                pe.wait_ge(da_wt, hd + 1)
                o = bank(6 + hd // 2)[:, (hd % 2) * T:(hd % 2 + 1) * T]
                w = wT[:, hd % 2, :]
                v = va3[:, :, hd * P:(hd + 1) * P]
                mm(o[:, 0:P], w[:, 0:P], v[:, 0], start=True, stop=True)
                mm(o[:, P:T], w[:, P:T], v[:, 0], start=True, stop=False)
                mm(o[:, P:T], w[:, T:BLOCKS], v[:, 1], start=False, stop=True).then_inc(da_o, 1)

            pe.wait_ge(evac[VA], 1)
            transpose_weights(0)
            transpose_weights(1)
            head_values(0)
            transpose_weights(2)
            head_values(1)
            transpose_weights(3)
            head_values(2)
            head_values(3)
            wait_slot(10)
            pe.wait_ge(evac[GB0], 1)
            pe.wait_ge(evac[GB1], 1)

            def project_out(n, first_bank, heads, done):
                w = slot(n % RING, 4, D)
                for j in range(KC):
                    for c in range(4):
                        last = mm(bank(first_bank + j // 2)[:, (j % 2) * T:(j % 2 + 1) * T], w[:, c, j * P:(j + 1) * P],
                                  heads[:, c, :], start=c == 0, stop=c == 3)
                    if j % 2:
                        last.then_inc(done, 1)

            project_out(10, 0, obT, yb_done)
            pe.wait_ge(on_ready, 1)
            for hd in range(DA_HEADS):
                for a in range(NT):
                    c0 = (hd % 2) * T + a * P
                    last = nc.tensor.transpose(bank(4 + hd // 2)[:, c0:c0 + P], on3[:, a, hd * P:(hd + 1) * P], ident)
            last.then_inc(tro, 1)
            wait_slot(11)
            pe.wait_ge(oT_act, 1)
            pe.wait_ge(oT_dve, 1)
            project_out(11, 4, oT, ya_done)
            wait_slot(12)
            wait_slot(13)

            def router_transposes(a, halves):
                for b in halves:
                    for c in range(4):
                        lo = (4 * b + c) * P
                        last = nc.tensor.transpose(bank(4 + 2 * a + b)[:, c * P:(c + 1) * P], x3[:, a, lo:lo + P], ident)
                    last.then_inc(tx_done, 1)

            def router_logits(a, halves):
                for c in (4 * b + c for b in halves for c in range(4)):
                    last = mm(bank(4 * a)[0:E, 0:P], wr3[:, c, :], hTr[a][:, c, :], start=c == 0, stop=c == KC - 1)
                if 1 in halves:
                    last.then_inc(rt_done, 1)

            def router_back(a):
                pe.wait_ge(lT_ready, a + 1)
                nc.tensor.transpose(bank(1 + 4 * a)[:, 0:E], lT[0:E, a * P:(a + 1) * P], ident[0:E, 0:E]).then_inc(rt_tr, 1)

            def out_weights(j, half):
                return slot((12 + half) % RING, KC, W512)[:, j, :]

            for j in range(KC):
                pe.wait_ge(mix_ready, j // 2 + 1)
                for half in range(2):
                    last = mm(bank(half), mixT[:, j, 0:P], out_weights(j, half), start=j == 0, stop=j == KC - 1)
            last.then_inc(wo_done, 1)
            for half in range(2):
                for j in range(KC):
                    last = mm(bank(2 + half), mixT[:, j, P:T], out_weights(j, half), start=j == 0, stop=j == KC - 1)
                    if (half, j) == (0, 2):
                        pe.wait_ge(x1, 1)
                        router_transposes(0, (0, 1))
                    if (half, j) == (0, 6):
                        pe.wait_ge(hTr_dve, 1)
                        pe.wait_ge(hTr_act, 1)
                        router_logits(0, (0, 1))
                    if (half, j) == (1, 1):
                        router_back(0)
                        pe.wait_ge(x1, 2)
                        router_transposes(1, (0,))
                    if (half, j) == (1, 5):
                        pe.wait_ge(hTr_act, 2)
                        router_logits(1, (0,))
                last.then_inc(wo_done, 1)
            pe.wait_ge(x1, 3)
            router_transposes(1, (1,))
            pe.wait_ge(hTr_dve, 2)
            router_logits(1, (1,))
            r = bank(2)
            pe.wait_ge(mask_ready, 1)
            mm(r[:, 0:E], su_b[:, :], mask_b[:, 0, :], start=True, stop=True)
            router_back(1)
            pe.wait_ge(mask_ready, 2)
            mm(r[:, E:2 * E], one_b[:, :], mask_b[:, 0, :], start=True, stop=False)
            mm(r[:, E:2 * E], su_b[:, :], mask_b[:, 1, :], start=False, stop=True)
            mm(r[:, 2 * E:3 * E], one_b[:, :], mask_b[:, 0, :], start=True, stop=False)
            mm(r[:, 2 * E:3 * E], one_b[:, :], mask_b[:, 1, :], start=False, stop=True).then_inc(rk_done, 1)

            def gather(n_value, first=False):
                pe.wait_ge(sel_ready, n_value)
                for c in range(KC):
                    if first and c % 4 == 0:
                        pe.wait_ge(h_ready, 2 + c // 4 + 1)
                    for k, (a, w) in enumerate((a, w) for a in range(NT) for w in range(3)):
                        last = mm(bank(T_B + c // 4)[:, (c % 4) * P:(c % 4 + 1) * P], h3[:, a, w, c, :],
                                  s_sel[:, a, :], start=k == 0, stop=k == 2 * 3 - 1)
                    if c % 4 == 3:
                        last.then_inc(gat_done, 1)

            gather(1, first=True)
            pe.wait_ge(ld_bias3, 16 * 12)

            def expert_iteration(i, it):
                for q in range(PAIRS_PER_ITER):
                    n = it * PAIRS_PER_ITER + q

                    def loaded(m):
                        p = LOADS_PER_PAIR * q + m
                        b = SLOT_OF[p]
                        before = len(range(b, HEAD_LOADS, RING)) if b < RING else 0
                        signals = [16 * DMAS_OF[x] for x in range(LOADS_PER_ITER) if SLOT_OF[x] == b]
                        pe.wait_ge(slot_loaded[b], it * sum(signals)
                                   + 16 * before + sum(signals[:SLOT_OF[:p + 1].count(b)]))
                        return [expert_part(b, k).rearrange("p (c n) -> p c n", c=2) for k in range(2)]

                    def biases(which, banks):
                        for half in range(2):
                            mm(bank(banks + half), oh[q][0:3 * E, :], bias3[0:3 * E, which, half * W512:(half + 1) * W512],
                               start=True, stop=False, skip_group_check=True)

                    def gate_or_up(which, banks):
                        biases(which, banks)
                        for m in range(4):
                            w = loaded(4 * which + m)
                            if which == 0 and m % 2 == 0:
                                pe.wait_ge(xT_ready, n * 2 + 1 + m // 2)
                            for c in range(2):
                                for half in range(2):
                                    for k in range(2):
                                        rows = slice(k * SLOTS, (k + 1) * SLOTS)
                                        last = mm(bank(banks + half)[rows, :], xT[:, 2 * m + c, rows],
                                                  w[k][:, c, half * W512:(half + 1) * W512], start=False,
                                                  stop=m == 3 and c == 1, skip_group_check=True)
                            last.then_inc(load_used, 1)

                    pe.wait_ge(sel_ready, n + 1)
                    gate_or_up(0, G_B)
                    pe.wait_ge(y_added, n * 4 + 1)
                    gate_or_up(1, U_B)
                    gather(n + 2)
                    pe.wait_ge(gs_ready, n + 1)
                    for a in range(NT):
                        last = nc.tensor.transpose(bank(O_B)[:, a * P:(a + 1) * P], gs[:, a, :], ident)
                    last.then_inc(gt_done, 1)
                    pe.wait_ge(xT_ready, n * 2 + 4)
                    pe.wait_ge(act_ready, n + 1)
                    for b in range(2):
                        for c in range(4):
                            last = nc.tensor.transpose(bank(T_B + b)[:, c * P:(c + 1) * P],
                                                       g_s[:, b * W512 + c:(b + 1) * W512:4], ident)
                        last.then_inc(ht_done, 1)
                    pe.wait_ge(gt_ready, n + 1)
                    biases(2, O_B)
                    def down(w, m, half, c):
                        for k in range(2):
                            rows = slice(k * SLOTS, (k + 1) * SLOTS)
                            last = mm(bank(O_B + half)[rows, :], hTm[:, 2 * m + c, rows],
                                      w[k][:, c, half * W512:(half + 1) * W512], start=False,
                                      stop=m == 3 and c == 1, skip_group_check=True)
                        return last

                    def scatter(half, b):
                        pe.wait_ge(o_ready, n * 2 + half + 1)
                        for a in range(NT):
                            last = mm(bank(b + a), g_T[:, a * P:(a + 1) * P], o_s[:, half * W512:(half + 1) * W512],
                                      start=True, stop=True)
                        last.then_inc(sc_done, 1)

                    for m in range(3):
                        w = loaded(8 + m)
                        pe.wait_ge(hT_ready, n * 2 + m // 2 + 1)
                        for c in range(2):
                            for half in range(2):
                                last = down(w, m, half, c)
                        last.then_inc(load_used, 1)
                    w = loaded(11)
                    for c in range(2):
                        last = down(w, 3, 0, c)
                    last.then_inc(down_done, 1)
                    pe.wait_ge(half_loaded[SLOT_OF[LOADS_PER_PAIR * q + 11]], it * 32 + 32)
                    for c in range(2):
                        last = down(w, 3, 1, c)
                    last.then_inc(load_used, 1)
                    scatter(0, U_B)
                    scatter(1, T_B)

            with pe.Fori(0, ITERS) as i:
                expert_iteration(i, i)
            rounds_after_first(pe, expert_iteration)


_INS = ["x", "norm_mix_g", "w_in", "lambda_q1", "lambda_k1", "lambda_q2", "lambda_k2", "da_subln_g", "w_da_out",
        "w_sb_out", "w_o", "norm_ffn_g", "w_router", "b_router", "w_gate", "b_gate", "w_up", "b_up", "w_down",
        "b_down", "norm_final_g"]
_SQUEEZED = {"x", "w_in", "w_da_out", "w_sb_out", "w_o", "w_router", "w_gate", "b_gate", "w_up", "b_up", "w_down",
             "b_down"}


def kernel(**inputs):
    import concourse.bacc as bacc
    from concourse.bass_utils import run_bass_kernel_spmd

    nc = bacc.Bacc("TRN2", target_bir_lowering=False, num_devices=1, dynamic_dma_scratch_size=1024)
    arrays, args = {}, []
    for name in _INS:
        a = np.ascontiguousarray(inputs[name])
        if name in _SQUEEZED:
            a = a.reshape(a.shape[1:])
        arrays[f"in_{name}"] = a
        args.append(nc.dram_tensor(f"in_{name}", a.shape, mybir.dt.from_np(a.dtype), kind="ExternalInput").ap())
    arrays["in_const"] = constants()
    args.append(nc.dram_tensor("in_const", arrays["in_const"].shape, F32, kind="ExternalInput").ap())
    args.append(nc.dram_tensor("out", (T, D), F32, kind="ExternalOutput").ap())
    build(nc, *args)
    r = run_bass_kernel_spmd(nc, [arrays], core_ids=[0])
    return r.results[0]["out"].reshape(1, T, D)
```
